# Optimizing a Trainium2 kernel written in Bass

```python
import jax, jax.numpy as jnp
from jax import lax
import numpy as np

D_MODEL = 1024
BATCH = 1
SEQ = 1024
DEPTH = 1

N_HEADS = 8
HEAD_DIM = 64
ATTN_WIDTH = N_HEADS * HEAD_DIM
CONV_CH = D_MODEL - ATTN_WIDTH
IN_COLS = 2 * CONV_CH + 3 * ATTN_WIDTH
CONV_WIDTH = 31
ROT_DIM = HEAD_DIM // 4
ROPE_THETA = 500000.0
DILATED_PATTERNS = ((128, 1), (512, 4), (2048, 16))
N_EXPERTS = 32
TOP_K = 4
D_FF = D_MODEL
SWIGLU_LIMIT = 7.0
SWIGLU_ALPHA = 1.702
MOE_BLOCK = 128
NORM_EPS = 1e-6

kernel_name = "hybrid_conv_dilated_attn_moe_adaln"

F32 = jnp.float32

def rms_norm(x, g):
    xf = x.astype(F32)
    y = xf * lax.rsqrt(jnp.mean(xf * xf, axis=-1, keepdims=True) + NORM_EPS)
    return (y * g.astype(F32)).astype(x.dtype)

def modulate(h, shift, scale):
    return h * (1.0 + scale) + shift

def rotary_tables(positions):
    inv_freq = ROPE_THETA ** (-jnp.arange(0, ROT_DIM, 2, dtype=F32) / ROT_DIM)
    ang = positions.astype(F32)[..., None] * inv_freq
    return jnp.cos(ang)[:, :, None, :], jnp.sin(ang)[:, :, None, :]

def apply_partial_rotary(t, cos, sin):
    half = ROT_DIM // 2
    tf = t.astype(F32)
    x1, x2, rest = tf[..., :half], tf[..., half:ROT_DIM], tf[..., ROT_DIM:]
    rot = jnp.concatenate([x1 * cos - x2 * sin, x2 * cos + x1 * sin, rest], axis=-1)
    return rot.astype(t.dtype)

def conformer_conv(a, g, conv_w, conv_b, ln_g, ln_b):
    u = a * jax.nn.sigmoid(g)
    y = lax.conv_general_dilated(
        u, conv_w.astype(u.dtype), window_strides=(1,),
        padding=[(CONV_WIDTH - 1, 0)],
        dimension_numbers=("NWC", "WIO", "NWC"),
        feature_group_count=CONV_CH) + conv_b
    yf = y.astype(F32)
    mu = jnp.mean(yf, axis=-1, keepdims=True)
    var = jnp.mean(jnp.square(yf - mu), axis=-1, keepdims=True)
    yn = (yf - mu) * lax.rsqrt(var + NORM_EPS) * ln_g.astype(F32) + ln_b.astype(F32)
    return jax.nn.silu(yn).astype(a.dtype)

def dilated_window_attention(q, k, v, window, dilation):
    Bb, S, H, hd = q.shape
    blk = window // dilation
    chunk = blk * dilation
    Sp = -(-S // chunk) * chunk
    L = Sp // dilation
    nb = L // blk

    def to_sub(t):
        t = jnp.pad(t, ((0, 0), (0, Sp - S), (0, 0), (0, 0)))
        t = t.reshape(Bb, L, dilation, H, hd).transpose(0, 2, 3, 1, 4)
        return t.reshape(Bb, dilation, H, nb, blk, hd)

    def with_prev(t):
        prev = jnp.pad(t, ((0, 0), (0, 0), (0, 0), (1, 0), (0, 0), (0, 0)))[:, :, :, :-1]
        return jnp.concatenate([prev, t], axis=4)

    qs = to_sub(q)
    ks = with_prev(to_sub(k))
    vs = with_prev(to_sub(v))
    s = jnp.einsum("bdhnqe,bdhnke->bdhnqk", qs.astype(F32), ks.astype(F32)) * (HEAD_DIM ** -0.5)
    qi = jnp.arange(blk)[:, None]
    kj = jnp.arange(2 * blk)[None, :]
    dist = qi + blk - kj
    band = (dist >= 0) & (dist <= blk)
    valid = band[None] & ((jnp.arange(nb)[:, None, None] > 0) | (kj >= blk)[None])
    s = jnp.where(valid, s, -jnp.inf)
    m = jnp.max(s, axis=-1)
    p = jnp.exp(s - m[..., None])
    l = jnp.sum(p, axis=-1)
    o = jnp.einsum("bdhnqk,bdhnke->bdhnqe", p, vs.astype(F32)) / l[..., None]

    o = o.reshape(Bb, dilation, H, L, hd).transpose(0, 3, 1, 2, 4).reshape(Bb, Sp, H, hd)[:, :S]
    m = m.reshape(Bb, dilation, H, L).transpose(0, 3, 1, 2).reshape(Bb, Sp, H)[:, :S]
    l = l.reshape(Bb, dilation, H, L).transpose(0, 3, 1, 2).reshape(Bb, Sp, H)[:, :S]
    return o, m, l

def dilated_mixture_attention(q, k, v):
    res = [dilated_window_attention(q, k, v, w, d) for (w, d) in DILATED_PATTERNS]
    m_all = jnp.max(jnp.stack([r[1] for r in res], axis=0), axis=0)
    wts = [jnp.exp(r[1] - m_all) * r[2] for r in res]
    num = sum(w[..., None] * r[0] for w, r in zip(wts, res))
    den = sum(wts)
    return num / den[..., None]

def routed_ffn(h, w_router, b_router, w_gu, b_gu, w_down, b_down):
    Bb, S, D = h.shape
    T = Bb * S
    hf = h.reshape(T, D)
    logits = hf.astype(F32) @ w_router.astype(F32) + b_router.astype(F32)
    top_val, top_idx = lax.top_k(logits, TOP_K)
    gates = jax.nn.softmax(top_val, axis=-1)

    A = T * TOP_K
    e_flat = top_idx.reshape(A).astype(jnp.int32)
    tok_flat = jnp.repeat(jnp.arange(T, dtype=jnp.int32), TOP_K)
    g_flat = gates.reshape(A)
    e_sorted, order = lax.sort((e_flat, jnp.arange(A, dtype=jnp.int32)), num_keys=1, is_stable=True)
    counts = jnp.bincount(e_flat, length=N_EXPERTS).astype(jnp.int32)
    starts = jnp.cumsum(counts) - counts
    padded = (counts + MOE_BLOCK - 1) // MOE_BLOCK * MOE_BLOCK
    pends = jnp.cumsum(padded)
    pstarts = pends - padded
    dest = pstarts[e_sorted] + (jnp.arange(A, dtype=jnp.int32) - starts[e_sorted])
    n_blocks = -(-A // MOE_BLOCK) + N_EXPERTS
    rows = n_blocks * MOE_BLOCK
    tok_pad = jnp.full((rows,), T, jnp.int32).at[dest].set(tok_flat[order])
    gate_pad = jnp.zeros((rows,), h.dtype).at[dest].set(g_flat[order].astype(h.dtype))
    block_start = jnp.arange(n_blocks, dtype=jnp.int32) * MOE_BLOCK
    block_expert = jnp.minimum(jnp.searchsorted(pends, block_start, side="right"), N_EXPERTS - 1).astype(jnp.int32)
    h_ext = jnp.concatenate([hf, jnp.zeros((1, D), hf.dtype)], axis=0)

    def expert_block(args):
        tok, e = args
        xb = h_ext[tok]
        gu = xb @ w_gu[e] + b_gu[e]
        gate = jnp.minimum(gu[:, :D_FF], SWIGLU_LIMIT)
        up = jnp.clip(gu[:, D_FF:], -SWIGLU_LIMIT, SWIGLU_LIMIT)
        act = (up + 1.0) * (gate * jax.nn.sigmoid(SWIGLU_ALPHA * gate))
        return act @ w_down[e] + b_down[e]

    y = lax.map(expert_block, (tok_pad.reshape(n_blocks, MOE_BLOCK), block_expert))
    y = y.reshape(rows, D) * gate_pad[:, None]
    out = jnp.zeros((T + 1, D), y.dtype).at[tok_pad].add(y)[:T]
    return out.reshape(Bb, S, D).astype(h.dtype)

def setup_inputs(seed: int = 0) -> dict:
    key = jax.random.key(seed)
    ks = jax.random.split(key, 24)

    def nrm(k, shape, scale):
        return jax.random.normal(k, shape, F32) * scale

    x = nrm(ks[0], (BATCH, SEQ, D_MODEL), 1.0)
    c = nrm(ks[1], (BATCH, D_MODEL), 1.0)
    positions = (jax.random.randint(ks[2], (BATCH, 1), 0, 4096, dtype=jnp.int32)
                 + jnp.arange(SEQ, dtype=jnp.int32)[None, :])
    return {
        "x": x,
        "c": c,
        "positions": positions,
        "w_ada": nrm(ks[3], (DEPTH, D_MODEL, 6 * D_MODEL), 0.5 * D_MODEL ** -0.5),
        "b_ada": nrm(ks[4], (DEPTH, 6 * D_MODEL), 0.02),
        "g_mix": 1.0 + nrm(ks[5], (DEPTH, D_MODEL), 0.05),
        "w_in": nrm(ks[6], (DEPTH, D_MODEL, IN_COLS), D_MODEL ** -0.5),
        "conv_w": nrm(ks[7], (DEPTH, CONV_WIDTH, 1, CONV_CH), CONV_WIDTH ** -0.5),
        "conv_b": nrm(ks[8], (DEPTH, CONV_CH), 0.02),
        "conv_ln_g": 1.0 + nrm(ks[9], (DEPTH, CONV_CH), 0.05),
        "conv_ln_b": nrm(ks[10], (DEPTH, CONV_CH), 0.02),
        "w_out": nrm(ks[11], (DEPTH, D_MODEL, D_MODEL), D_MODEL ** -0.5),
        "g_ffn": 1.0 + nrm(ks[12], (DEPTH, D_MODEL), 0.05),
        "w_router": nrm(ks[13], (DEPTH, D_MODEL, N_EXPERTS), D_MODEL ** -0.5),
        "b_router": nrm(ks[14], (DEPTH, N_EXPERTS), 0.01),
        "w_gu": nrm(ks[15], (DEPTH, N_EXPERTS, D_MODEL, 2 * D_FF), D_MODEL ** -0.5),
        "b_gu": nrm(ks[16], (DEPTH, N_EXPERTS, 2 * D_FF), 0.02),
        "w_down": nrm(ks[17], (DEPTH, N_EXPERTS, D_FF, D_MODEL), D_FF ** -0.5),
        "b_down": nrm(ks[18], (DEPTH, N_EXPERTS, D_MODEL), 0.02),
        "g_final": 1.0 + nrm(ks[19], (D_MODEL,), 0.05),
    }

def reference(x, c, positions, w_ada, b_ada, g_mix, w_in, conv_w, conv_b, conv_ln_g, conv_ln_b,
              w_out, g_ffn, w_router, b_router, w_gu, b_gu, w_down, b_down, g_final):
    Bb, S, _ = x.shape
    cos, sin = rotary_tables(positions)
    c_act = jax.nn.silu(c)
    splits = [CONV_CH, 2 * CONV_CH, 2 * CONV_CH + ATTN_WIDTH, 2 * CONV_CH + 2 * ATTN_WIDTH]
    for l in range(DEPTH):
        mod = (c_act @ w_ada[l] + b_ada[l])[:, None, :]
        sh1, sc1, gt1, sh2, sc2, gt2 = jnp.split(mod, 6, axis=-1)

        h = modulate(rms_norm(x, g_mix[l]), sh1, sc1)
        proj = h @ w_in[l]
        a, g, q, k, v = jnp.split(proj, splits, axis=-1)
        conv_out = conformer_conv(a, g, conv_w[l], conv_b[l], conv_ln_g[l], conv_ln_b[l])
        q = apply_partial_rotary(q.reshape(Bb, S, N_HEADS, HEAD_DIM), cos, sin)
        k = apply_partial_rotary(k.reshape(Bb, S, N_HEADS, HEAD_DIM), cos, sin)
        v = v.reshape(Bb, S, N_HEADS, HEAD_DIM)
        attn_out = dilated_mixture_attention(q, k, v).reshape(Bb, S, ATTN_WIDTH).astype(x.dtype)
        mixed = jnp.concatenate([conv_out, attn_out], axis=-1) @ w_out[l]
        x = x + gt1 * mixed

        h2 = modulate(rms_norm(x, g_ffn[l]), sh2, sc2)
        x = x + gt2 * routed_ffn(h2, w_router[l], b_router[l], w_gu[l], b_gu[l], w_down[l], b_down[l])
    return rms_norm(x, g_final)


_drawn_inputs = setup_inputs


def setup_inputs(seed=0):
    import zlib

    import numpy as np

    out = dict(_drawn_inputs(seed))
    spreads = {}
    factors = {'g_mix': 3.934,
     'conv_b': 6.215,
     'conv_ln_g': 4.508,
     'conv_ln_b': 21.65,
     'b_router': 13.891,
     'b_gu': 8.0,
     'b_down': 24.442,
     'g_ffn': 2.859}
    for name, (base, spread) in spreads.items():
        noise = np.random.default_rng([zlib.crc32(name.encode()), seed]).standard_normal(out[name].shape)
        drawn = base * np.exp(spread * noise) if base else spread * noise
        out[name] = __import__('jax').numpy.asarray(drawn.astype(out[name].dtype))
    for name, factor in factors.items():
        out[name] = (out[name] * factor).astype(out[name].dtype)
    return out
```

```python
import math
from contextlib import ExitStack

import numpy as np

import concourse.bass as bass
from concourse import mybir

F32 = mybir.dt.float32
BF16 = mybir.dt.bfloat16
I32 = mybir.dt.int32
U32 = mybir.dt.uint32
ALU = mybir.AluOpType
ACT = mybir.ActivationFunctionType
AX_X = mybir.AxisListType.X

P = 128
T = 1024
TT = T // P
D = 1024
KD = D // P
HALF = 512
CH = 512
CT = CH // P
TAPS = 31
PADDED = T + TAPS - 1
HEADS = 8
HD = 64
ROT = 16
THETA = 500000.0
QT = HEADS * HD // P
NE = 32
TOPK = 4
LIMIT = 7.0
ALPHA = 1.702
EPS = 1e-6
PIECE = 256
SLOTS = 256
CLASSES = SLOTS // 64
MORE = 16
VISITS = NE + MORE
NEVER = 8192.0
RING = 12
RING1 = 8
BIG = 1e30
FT = D // P
LINKS_PER_VISIT = 7
ROUND = 12582912.0
TWO_PI_A = 6.28125
TWO_PI_B = float(np.float32(round((2 * math.pi - 6.28125) * 2**20) / 2**20))
TWO_PI_C = float(2 * math.pi - TWO_PI_A - TWO_PI_B)


class Chain:

    def __init__(self, engine, sem):
        self.engine, self.sem, self.count, self.base = engine, sem, 0, 0

    def loop(self, turn, per):
        self.start, self.per = self.count, per
        self.base = turn * per

    def end(self, times):
        assert self.count - self.start == self.per, (self.count - self.start, self.per)
        self.base = (times - 1) * self.per

    def mark(self, ins):
        self.count += 1
        ins.then_inc(self.sem, 1)

    def wait(self):
        self.engine.wait_ge(self.sem, self.base + self.count)

    def __call__(self, ins):
        self.mark(ins)
        self.wait()


def decoder_layer(nc, x, c, positions, w_ada, b_ada, g_mix, w_in, conv_w, conv_b, conv_ln_g, conv_ln_b,
                  w_out, g_ffn, w_router, b_router, w_gu, b_gu, w_down, b_down, g_final, out):
    ctx = ExitStack()
    with ctx:
        def sb(name, shape, dt=F32):
            return ctx.enter_context(nc.sbuf_tensor(name, shape, dt))

        def sem(name):
            return ctx.enter_context(nc.semaphore(name))

        xn_rows = nc.dram_tensor("xn_rows", (T, D), F32).ap()
        sum_rows = nc.dram_tensor("sum_rows", (T + SLOTS, D), F32).ap()

        ring = sb("ring", [P, RING, KD, PIECE])
        high = ring[:, RING1:RING].rearrange("p s k n -> p (s k n)")
        qT = high[:, 0:QT * T].rearrange("p (f t) -> p f t", f=QT)
        kT = high[:, QT * T:2 * QT * T].rearrange("p (f t) -> p f t", f=QT)

        at_h = 0
        at_u = at_h + KD * T
        at_y = at_u + CT * PADDED
        at_v = at_y + CT * T
        at_trig = at_v + TT * HALF
        at_mask = at_trig + 2 * T
        arena = sb("arena", [P, at_mask + T])

        def part(start, size, **dims):
            view = arena[:, start:start + size]
            if dims:
                (name, n), = dims.items()
                view = view.rearrange(f"p ({name} n) -> p {name} n", **{name: n})
            return view

        hT = part(at_h, KD * T, k=KD)
        row_a, row_c, freq_row = (part(at_h + 4096 + i * P, P) for i in range(3))
        row_g = part(at_h + 4608, 4 * P, q=4)
        iota_i = part(at_h + 5120, SLOTS).bitcast(I32)
        u_pad = part(at_u, CT * PADDED, c=CT)
        conv = part(at_y, CT * T, c=CT)
        x_in = part(at_y, TT * D, t=TT)
        sig_g = part(at_v, CT * T, c=CT)
        v_nat = part(at_v, TT * HALF, t=TT)
        cos_t, sin_t = part(at_trig, T), part(at_trig + T, T)
        mask = part(at_mask, T)
        tmp = [part(at_u + i * T, T) for i in range(4)]
        rot_tmp = [part(at_u + i * HALF, HALF) for i in range(2)]
        norm_tmp = [part(at_u + i * T, T) for i in range(4)]
        attnT = part(at_h, QT * T, f=QT)
        prob = [part(at_h + 4096 + i * T, T) for i in range(2)]
        probT = [part(at_h + 6144 + i * T, T) for i in range(2)]
        o_nat = [part(at_trig + i * HALF, HALF) for i in range(2)]
        x_again = part(at_u, 2 * D, t=2)
        x1 = [part(at_h + 4096 + i * D, D) for i in range(2)]
        xn1 = [part(at_h + 6144 + i * D, D) for i in range(2)]
        h2T = [part(at_v + i * D, D, k=KD) for i in range(2)]
        acc_sb = [part(at_v + 2 * D + i * D, D) for i in range(2)]
        square = part(at_trig, D)
        b_down_sb = arena[0:NE, at_trig + D:at_trig + 2 * D]
        gate2_b = part(at_u + 2 * D, D)
        g_cols = part(at_u + 3 * D, TT * NE * 4).bitcast(BF16).rearrange("p (t e n) -> p t e n", t=TT, e=NE)
        gates = part(at_mask, TT * NE, t=TT)
        place = part(at_mask + TT * NE, TT * NE, t=TT)
        g_rest = part(at_mask + 2 * TT * NE, TT * NE, t=TT)
        is_before = part(at_y, MORE * NE, o=MORE)
        more_before = part(at_y + MORE * NE, MORE * NE, o=MORE)
        xT = part(at_v, KD * SLOTS, k=KD)
        got = [part(at_v + 2 * D + b * D, D) for b in range(2)]
        actT = part(at_y, FT * SLOTS, k=FT)
        yT = part(at_y + FT * SLOTS, KD * SLOTS, k=KD)
        y_nat = [part(at_h + b * D, D) for b in range(2)]
        onehot = part(at_h + 2 * D, TT * SLOTS // 2).bitcast(BF16).rearrange("p (t n) -> p t n", t=TT)
        g_buf, u_buf, s_buf, t_buf = (part(at_h + 3 * D + i * 2 * SLOTS, 2 * SLOTS, k=2) for i in range(4))
        fin = part(at_u, 4 * D, t=4)
        fin_square = part(at_y, D)
        g_fin_b = part(at_v, D)

        ident = sb("ident", [P, P])
        ones = sb("ones", [P, P])
        rot_m = sb("rot_m", [P, P])
        before_m = sb("before_m", [P, P], BF16)
        ones_b = sb("ones_b", [P, P], BF16)
        cols = sb("cols", [P, 84])
        C_ADA, C_MIX, C_FFN, C_CB, C_LG, C_LB = 8, 56, 64, 72, 76, 80
        conv_cols = sb("conv_cols", [P, TAPS * CT])
        bgu = sb("bgu", [P, NE, 2 * FT])
        c_sigm = sb("c_sigm", [P, KD])
        c_act = sb("c_act", [P, KD])
        c_bc = sb("c_bc", [P, KD, P])
        mod1 = sb("mod1", [P, 2 * KD])
        mod2 = sb("mod2", [P, 2 * KD])
        scale1 = sb("scale1", [P, KD])
        scale2 = sb("scale2", [P, KD])
        gate1_b = sb("gate1_b", [P, D])
        freq = sb("freq", [P, 1])
        settled = sb("settled", [1, 1])
        minus_half = sb("minus_half", [P, 1])
        ssq = sb("ssq", [P, TT])
        mean_sq = sb("mean_sq", [P, TT])
        rstd = sb("rstd", [P, TT])
        ssq2 = sb("ssq2", [P, TT])
        mean_sq2 = sb("mean_sq2", [P, TT])
        rstd2 = sb("rstd2", [P, TT])
        ssq3 = sb("ssq3", [P, TT])
        mean_sq3 = sb("mean_sq3", [P, TT])
        rstd3 = sb("rstd3", [P, TT])
        soft = sb("soft", [P, 4, 4])
        wr = sb("wr", [P, KD, NE])
        br = sb("br", [P, NE])
        iota_f = sb("iota_f", [P, NE])
        iota_b = sb("iota_b", [P, SLOTS], BF16)
        logit = sb("logit", [P, NE])
        top = sb("top", [P, 2, 8])
        top_i = sb("top_i", [P, 8], U32)
        top_f = sb("top_f", [P, 8])
        top_e = sb("top_e", [P, 2, 8])
        gate4 = sb("gate4", [P, TOPK])
        hit = sb("hit", [P, NE])
        picked = sb("picked", [P, 2, NE])
        picked_b = sb("picked_b", [P, 2, NE], BF16)
        so_far = sb("so_far", [P, NE])
        so_far_b = sb("so_far_b", [P, 2, NE], BF16)
        gatesT = sb("gatesT", [NE, P])
        place_e = sb("place_e", [P, TT])
        g_e = sb("g_e", [P, TT, 8], BF16)
        bias_e = sb("bias_e", [P, 2 * FT])
        pool_i = sb("pool_i", [P, 2], I32)
        slot_id = sb("slot_id", [P, 2])
        list_sb = sb("list_sb", [P, 2, 8])
        look = sb("look", [P, 2, 2])
        here = sb("here", [P, 2, 2])
        gone_g = sb("gone_g", [P, 2])
        gather_i = sb("gather_i", [P, 2], I32)
        scatter_i = sb("scatter_i", [P, 2], I32)
        cnt = sb("cnt", [P, NE])
        more_e = sb("more_e", [P, NE])
        incl = sb("incl", [P, NE])
        v_tab = sb("v_tab", [P, 3, VISITS + 1])
        v_int = sb("v_int", [P, 2, VISITS + 1], I32)
        o_tmp = sb("o_tmp", [P, 4, MORE])
        n_vis = sb("n_vis", [P, 1], I32)

        bank = [ctx.enter_context(nc.psum_tensor(f"bank{i}", [P, HALF], F32)) for i in range(4)]
        wide = [ctx.enter_context(nc.psum_tensor(f"wide{i}", [P, 2 * HALF], F32)) for i in range(2)]

        def half(i):
            return bank[i][:, :] if i < 4 else wide[(i - 4) // 2][:, (i % 2) * HALF:(i % 2 + 1) * HALF]

        list_ps = half(7)[:, 0:16].rearrange("p (b n) -> p b n", b=2)

        names = """small_loaded consts_made idents_made iotas_made chain_pool chain_dve 
            rows_turned cols_made c_sigmoid c_ready c_spread mod_summed scale1_made scale2_made gates_summed gate_made
            angles_made sines_made ssq_made rstd_made x_scaled x_turned h_even h_odd
            ag_summed a_copied sig_made u_made qkv_summed qkv_copied rot_summed rot_read q_rotated
            conv_made mean_summed centred squared var_summed var_made std_made z_made z_sigmoid conv_out
            scored score_masked exped prob_turned probT_act probT_dve weighed o_made attn_turned attn_made
            gate2_loaded b_down_loaded mixed mix_read x1_made ssq2_made rstd2_made xn_made xn_turned h2_low h2_high
            logits_summed top_made exp4_made picked_made gatesT_made bd_summed bd_read acc_made
            placed counted settles tables_ready zeros_made
            list_made list_summed gather_ready gathered_a gathered_b x2_turned x2_made
            pair_summed g_made pair_read t_made s_made act_made y_summed y_copied y_turned y_made
            scattered_a scattered_b g_final_loaded fin_ssq fin_rstd fin_made""".split()
        S = {n: sem(n) for n in names}
        dense_loaded = [sem(f"dense_loaded{i}") for i in range(RING1)]
        x_loaded = [sem(f"x_loaded{t}") for t in range(TT)]
        x_back = [sem(f"x_back{b}") for b in range(2)]
        xn_stored = [sem(f"xn_stored{b}") for b in range(2)]
        acc_stored = [sem(f"acc_stored{b}") for b in range(2)]
        fin_loaded = [sem(f"fin_loaded{b}") for b in range(4)]
        fin_stored = [sem(f"fin_stored{b}") for b in range(4)]
        piece_loaded = [sem(f"piece_loaded{i}") for i in range(RING)]

        def columns(w, first):
            return w[:, first:first + PIECE].rearrange("(k p) n -> p k n", p=P)

        def rows(v, n=P):
            return v.rearrange("(q p) -> q p", p=n)

        dense = [(columns(w_ada, i * PIECE), "mod_summed", i + 1) for i in range(8)]
        AG = len(dense)
        dense += [(columns(w_in, first), "ag_summed", used)
                  for first, used in ((0, 7), (CH, 8), (PIECE, 15), (CH + PIECE, 16))]
        QK = len(dense)
        dense += [(columns(w_in, 2 * CH + i * PIECE), "qkv_summed", min(4 * (i + 1), 24) if i < 4 else 24) for i in range(6)]
        ADA2 = len(dense)
        dense += [(columns(w_ada, (8 + i) * PIECE), "gates_summed", i + 1) for i in range(4)]
        dense += [(columns(w_ada, (12 + i) * PIECE), "mod_summed", 9 + i) for i in range(8)]
        dense += [(columns(w_ada, (20 + i) * PIECE), "gates_summed", 5 + i) for i in range(4)]
        OUT = len(dense)
        dense += [(columns(w_out, i * PIECE), "mixed", TT) for i in range(4)]

        def dense_piece(n):
            return ring[:, n % RING1]

        def ring_slot(i):
            return (i + 6) % RING

        block = ctx.enter_context(nc.Block())

        @block.sync
        def _(sp):
            for t in range(TT):
                sp.dma_start(x_in[:, t, :], x[t * P:(t + 1) * P, :]).then_inc(x_loaded[t], 16)
            for n, (src, _, _) in enumerate(dense):
                if n >= RING1:
                    sp.wait_ge(S[dense[n - RING1][1]], dense[n - RING1][2])
                sp.dma_start(dense_piece(n), src).then_inc(dense_loaded[n % RING1], 16)

            def expert_piece(e, i):
                w, first = (w_gu, (i // 2) * PIECE + (i % 2) * D) if i < 8 else (w_down, (i - 8) * PIECE)
                return w[bass.ds(e, 1), :, first:first + PIECE].rearrange("a (k p) n -> p (a k) n", p=P)

            for i in range(RING):
                slot = ring_slot(i)
                if slot < RING1:
                    last = max(n for n in range(len(dense)) if n % RING1 == slot)
                    sp.wait_ge(S[dense[last][1]], dense[last][2])
                else:
                    sp.wait_ge(S["scored"], TT * HEADS)
                sp.dma_start(ring[:, slot], expert_piece(0, i)).then_inc(piece_loaded[i], 16)
            sp.wait_ge(S["tables_ready"], 1)
            with sp.Fori(1, VISITS) as v:
                cls = sp.value_load(v_int[0:1, 1, bass.ds(v, 1)], min_val=0, max_val=CLASSES)
                with sp.If(cls > 0):
                    e = sp.value_load(v_int[0:1, 0, bass.ds(v, 1)], min_val=0, max_val=NE - 1)
                    for i in range(RING):
                        if i < 8:
                            sp.wait_ge(S["pair_summed"], v * FT + (2 * (i // 2 + 1) - FT))
                        else:
                            sp.wait_ge(S["y_summed"], v * KD + (2 * (i - 7) - KD))
                        sp.dma_start(ring[:, ring_slot(i)], expert_piece(e, i)).then_inc(piece_loaded[i], 16)
            for t in range(TT):
                sp.wait_ge(S["fin_made"], t + 1)
                sp.dma_start(out[t * P:(t + 1) * P, :], fin[:, t % 4, :]).then_inc(fin_stored[t % 4], 16)
            for b in range(4):
                sp.wait_ge(fin_stored[b], 16 * TT // 4)

        @block.gpsimd
        def _(pool):
            link = Chain(pool, S["chain_pool"])
            G = nc.gpsimd

            def diagonal(m, view, value, base, pattern):
                link(G.affine_select(out=view, in_=view, compare_op=ALU.not_equal, fill=value, base=base, pattern=pattern,
                                     channel_multiplier=1))

            link(G.memset(ident[:, :], 0.0))
            diagonal(ident, ident[:, :], 1.0, 0, [[-1, P]])
            G.memset(freq_row[0:1, :], 0.0)
            G.memset(minus_half[:, :], -0.5)
            link(G.memset(ones[:, :], 1.0))
            inv_freq = np.float32(THETA) ** (-(np.arange(0, ROT, 2, dtype=np.float32) / np.float32(ROT)))
            fr = freq_row[0:1, :].rearrange("a (h n) -> a h n", h=2)
            for j in range(ROT):
                ins = G.memset(fr[:, :, j:j + 1], float(inv_freq[j % (ROT // 2)]))
            ins.then_inc(S["idents_made"], 1)
            G.iota(tmp[3].bitcast(I32), pattern=[[-1, T]], base=T - P, channel_multiplier=1).then_inc(S["iotas_made"], 1)
            G.iota(iota_i, pattern=[[1, SLOTS]], base=0, channel_multiplier=0).then_inc(S["iotas_made"], 1)
            link(G.memset(rot_m[:, :], 0.0))
            rv = rot_m[:, :].rearrange("p (h n) -> p h n", h=2)
            diagonal(rot_m, rv[:, :, 0:8], -1.0, -8, [[-HD, 2], [-1, 8]])
            diagonal(rot_m, rv[:, :, 8:16], 1.0, 0, [[-HD, 2], [-1, 8]])
            link(G.memset(before_m[:, :], 1.0))
            link(G.affine_select(out=before_m[:, :], in_=before_m[:, :], compare_op=ALU.is_gt, fill=0.0, base=0,
                                 pattern=[[1, P]], channel_multiplier=-1))
            G.memset(ones_b[:, :], 1.0)
            link(G.iota(pool_i[:, :], pattern=[[P, 2]], base=T, channel_multiplier=1))
            link(G.tensor_copy(slot_id[:, :], pool_i[:, :]))
            G.memset(v_tab[:, 2, 0:NE], 0.0)
            G.memset(v_tab[:, 2, VISITS:VISITS + 1], NEVER)
            G.memset(v_tab[:, 0:2, VISITS:VISITS + 1], 0.0)
            G.memset(here[:, :, :], 0.0).then_inc(S["consts_made"], 1)

            def rsqrt_mean(t, sums, mean, result, ready, done):
                pool.wait_ge(S[ready], t + 1)
                link(G.tensor_scalar(mean[:, t:t + 1], sums[:, t:t + 1], 1.0 / D, EPS, ALU.mult, ALU.add))
                G.tensor_tensor(result[:, t:t + 1], mean[:, t:t + 1], minus_half[:, :], ALU.pow).then_inc(S[done], 1)

            for t in range(TT):
                rsqrt_mean(t, ssq, mean_sq, rstd, "ssq_made", "rstd_made")

            def reload(t):
                pool.dma_start(x_again[:, t % 2, :], x[t * P:(t + 1) * P, :]).then_inc(x_back[t % 2], 16)

            pool.wait_ge(S["conv_out"], CT)
            pool.dma_start(gate2_b, b_ada[5 * D:6 * D].partition_broadcast(P)).then_inc(S["gate2_loaded"], 16)
            rest_i = g_rest.rearrange("p t e -> p (t e)").bitcast(I32)
            pool.wait_ge(S["score_masked"], TT * HEADS)
            for col, pattern, step in ((0, [[0, TT * NE]], 1), (1, [[P, TT], [0, NE]], 0)):
                link(G.iota(rest_i, pattern=pattern, base=0, channel_multiplier=step))
                link(G.tensor_copy(g_cols[:, :, :, col], g_rest.bitcast(I32)))
            G.memset(g_cols[:, :, :, 2:3], 1.0)
            G.memset(g_cols[:, :, :, 6:8], 0.0).then_inc(S["consts_made"], 1)
            pool.wait_ge(S["attn_turned"], TT)
            pool.dma_start(b_down_sb, b_down).then_inc(S["b_down_loaded"], 16)
            reload(0)
            reload(1)
            pool.wait_ge(S["zeros_made"], 2)
            for b, done in enumerate(("scattered_a", "scattered_b")):
                pool.dma_start(sum_rows[T + b * P:T + (b + 1) * P, :], xn1[1]).then_inc(S[done], 16)
            for t in range(TT + 1):
                if t >= 2:
                    pool.wait_ge(S["acc_made"], t - 1)
                    pool.dma_start(sum_rows[(t - 2) * P:(t - 1) * P, :], acc_sb[t % 2]).then_inc(acc_stored[t % 2], 16)
                if t < TT:
                    rsqrt_mean(t, ssq2, mean_sq2, rstd2, "ssq2_made", "rstd2_made")
                    if t + 2 < TT:
                        reload(t + 2)
                    pool.wait_ge(S["xn_made"], t + 1)
                    pool.dma_start(xn_rows[t * P:(t + 1) * P, :], xn1[t % 2]).then_inc(xn_stored[t % 2], 16)
            pool.wait_ge(S["acc_made"], TT)
            pool.dma_start(sum_rows[(TT - 1) * P:TT * P, :], acc_sb[(TT - 1) % 2]).then_inc(acc_stored[(TT - 1) % 2], 16)
            for b in range(2):
                pool.wait_ge(xn_stored[b], 16 * TT // 2)
                pool.wait_ge(acc_stored[b], 16 * TT // 2)
            pool.wait_ge(S["scattered_a"], 16)
            pool.wait_ge(S["scattered_b"], 16)

            def settle(before=None):
                if before is not None:
                    pool.wait_ge(S["settles"], before)
                G.tensor_tensor(settled[:, :], minus_half[0:1, :], minus_half[0:1, :], ALU.add).then_inc(S["settles"], 1)

            def gather(n, before=None):
                pool.wait_ge(S["gather_ready"], n + 1)
                settle(before)
                for b, done in enumerate(("gathered_a", "gathered_b")):
                    pool.indirect_dma_start(got[b], None, xn_rows, bass.IndirectOffsetOnAxis(ap=gather_i[:, b:b + 1], axis=0),
                                            bounds_check=T - 1, oob_is_err=False).then_inc(S[done], 16)

            def scatter(n):
                for b, done in enumerate(("scattered_a", "scattered_b")):
                    pool.wait_ge(S["y_made"], n * 4 + (2 * b + 2))
                    settle(n * 3 + (b + 1))
                    pool.indirect_dma_start(sum_rows, bass.IndirectOffsetOnAxis(ap=scatter_i[:, b:b + 1], axis=0), y_nat[b], None,
                                            bounds_check=T + SLOTS - 1, oob_is_err=True, compute_op=ALU.add).then_inc(S[done], 16)

            gather(0)
            with pool.Fori(0, VISITS) as v:
                cls = pool.value_load(v_int[0:1, 1, bass.ds(v, 1)], min_val=0, max_val=CLASSES)
                with pool.If(cls > 0):
                    scatter(v)
                    gather(v + 1, v * 3 + 3)
            n = pool.value_load(n_vis[0:1, 0:1], min_val=NE, max_val=VISITS)
            scatter(n)
            pool.wait_ge(S["scattered_a"], n * 16 + 32)
            settle(n * 3 + 3)
            pool.wait_ge(S["scattered_b"], n * 16 + 32)
            settle(n * 3 + 4)
            pool.dma_start(g_fin_b, g_final.partition_broadcast(P)).then_inc(S["g_final_loaded"], 16)
            for t in range(TT):
                if t >= 4:
                    rsqrt_mean(t - 4, ssq3, mean_sq3, rstd3, "fin_ssq", "fin_rstd")
                    pool.wait_ge(fin_stored[t % 4], 16 * (t // 4))
                pool.dma_start(fin[:, t % 4, :], sum_rows[t * P:(t + 1) * P, :]).then_inc(fin_loaded[t % 4], 16)
            for t in range(TT - 4, TT):
                rsqrt_mean(t, ssq3, mean_sq3, rstd3, "fin_ssq", "fin_rstd")

        @block.scalar
        def _(act):
            A = nc.scalar
            first = 0
            for src, n in ((c, 8), (b_ada, 48), (g_mix, 8), (g_ffn, 8), (conv_b, 4), (conv_ln_g, 4), (conv_ln_b, 4)):
                act.dma_start(row_a[first:first + n, :], rows(src)).then_inc(S["small_loaded"], 16)
                first += n
            act.dma_start(row_c[0:TAPS * CT, :], rows(conv_w)).then_inc(S["small_loaded"], 16)
            act.dma_start(row_g[:, :, :], b_gu.rearrange("(q r p) -> r q p", r=P, p=P)).then_inc(S["small_loaded"], 16)
            act.dma_start(tmp[0].bitcast(I32), positions.partition_broadcast(P)).then_inc(S["small_loaded"], 16)
            act.dma_start(wr[:, :, :], w_router.rearrange("(k p) n -> p k n", p=P)).then_inc(S["small_loaded"], 16)
            act.dma_start(br[:, :], b_router.partition_broadcast(P)).then_inc(S["small_loaded"], 16)
            act.dma_start(gate1_b[:, :], b_ada[2 * D:3 * D].partition_broadcast(P)).then_inc(S["small_loaded"], 16)

            act.wait_ge(S["cols_made"], 1)
            A.activation(c_sigm[:, :], cols[:, 0:KD], ACT.Sigmoid).then_inc(S["c_sigmoid"], 1)
            for t in range(TT):
                act.wait_ge(x_loaded[t], 16)
                if t >= 1:
                    act.wait_ge(S["ssq_made"], t)
                A.activation(hT[:, 0, :], x_in[:, t, :], ACT.Square, accum_out=ssq[:, t:t + 1]).then_inc(S["ssq_made"], 1)
            act.wait_ge(S["angles_made"], 1)
            A.activation(sin_t, tmp[1], ACT.Sin)
            A.activation(cos_t, tmp[2], ACT.Sin).then_inc(S["sines_made"], 1)
            act.wait_ge(S["scale1_made"], 1)
            act.wait_ge(S["ssq_made"], TT)
            for n in range(0, 2 * KD, 2):
                g, k = n // KD, n % KD
                act.wait_ge(S["x_turned"], n + 1)
                A.activation(hT[:, k, g * HALF:(g + 1) * HALF], half(n % 4), ACT.Identity, scale=scale1[:, k:k + 1],
                             bias=mod1[:, k:k + 1]).then_inc(S["h_even"], 1)
            for i in range(2 * CT):
                ct, h = i // 2, i % 2
                act.wait_ge(S["ag_summed"], 2 * i + 1)
                A.copy(u_pad[:, ct, TAPS - 1 + h * HALF:TAPS - 1 + (h + 1) * HALF], half(4 + (2 * i) % 4)).then_inc(S["a_copied"], 1)
                act.wait_ge(S["ag_summed"], 2 * i + 2)
                A.activation(sig_g[:, ct, h * HALF:(h + 1) * HALF], half(4 + (2 * i + 1) % 4), ACT.Sigmoid).then_inc(S["sig_made"], 1)
            for i in range(4 * QT):
                dst, f = (qT, i // 2) if i < 2 * QT else (kT, i // 2 - QT)
                act.wait_ge(S["qkv_summed"], i + 1)
                A.copy(dst[:, f, (i % 2) * HALF:(i % 2 + 1) * HALF], half(i % 2)).then_inc(S["qkv_copied"], 1)
            act.wait_ge(S["u_made"], 2 * CT)
            for t in range(TT):
                act.wait_ge(S["qkv_summed"], 4 * QT + t + 1)
                A.copy(v_nat[:, t, :], half(t % 2)).then_inc(S["qkv_copied"], 1)
            for i in range(2 * CT):
                h, ct = i // CT, i % CT
                act.wait_ge(S["centred"], i + 1)
                if i >= 2:
                    act.wait_ge(S["var_summed"], i - 1)
                A.activation(norm_tmp[2 + i % 2][:, 0:HALF], conv[:, ct, h * HALF:(h + 1) * HALF], ACT.Square).then_inc(S["squared"], 1)
            act.wait_ge(S["var_made"], 1)
            A.activation(norm_tmp[0], norm_tmp[1], ACT.Sqrt).then_inc(S["std_made"], 1)
            for ct in range(CT):
                act.wait_ge(S["z_made"], ct + 1)
                if ct >= 2:
                    act.wait_ge(S["conv_out"], ct - 1)
                A.activation(norm_tmp[2 + ct % 2], conv[:, ct, :], ACT.Sigmoid).then_inc(S["z_sigmoid"], 1)

            def copy_turned(i):
                act.wait_ge(S["prob_turned"], i + 1)
                if i >= 2:
                    act.wait_ge(S["weighed"], i - 1)
                m = min((i // HEADS + 1) * P, HALF)
                A.copy(probT[i % 2][:, 0:m], half(0)[:, 0:m]).then_inc(S["probT_act"], 1)

            def copy_attn(qt):
                act.wait_ge(S["attn_turned"], qt + 1)
                A.copy(attnT[:, :, qt * P:(qt + 1) * P], half(3).rearrange("p (f t) -> p f t", f=QT)).then_inc(S["attn_made"], 1)

            ITEMS = TT * HEADS
            for i in range(ITEMS):
                n = (i // HEADS + 1) * P
                act.wait_ge(S["score_masked"], i + 1)
                A.activation(prob[i % 2][:, 0:n], prob[i % 2][:, 0:n], ACT.Exp, scale=HD ** -0.5, bias=soft[:, i % 4, 1:2],
                             accum_out=soft[:, i % 4, 2:3]).then_inc(S["exped"], 1)
                if i >= 1:
                    copy_turned(i - 1)
                if i > HEADS and i % HEADS == 4:
                    copy_attn(i // HEADS - 1)
            copy_turned(ITEMS - 1)
            copy_attn(TT - 1)

            for t in range(TT + 1):
                if t < TT:
                    act.wait_ge(S["x1_made"], t + 1)
                    if t >= 1:
                        act.wait_ge(S["ssq2_made"], t)
                    A.activation(square, x1[t % 2], ACT.Square, accum_out=ssq2[:, t:t + 1]).then_inc(S["ssq2_made"], 1)
                if t >= 1:
                    b = (t - 1) % 2
                    act.wait_ge(S["xn_turned"], t)
                    for k in range(KD // 2):
                        ins = A.activation(h2T[b][:, k, :], wide[1][:, k * P:(k + 1) * P], ACT.Identity, scale=scale2[:, k:k + 1],
                                           bias=mod2[:, k:k + 1])
                    ins.then_inc(S["h2_low"], 1)
                    act.wait_ge(S["top_made"], t)
                    A.activation(top_e[:, b, 0:TOPK], top[:, b, 0:TOPK], ACT.Exp, bias=top_e[:, b, 4:5],
                                 accum_out=top_e[:, b, 5:6]).then_inc(S["exp4_made"], 1)

            def turn_x(n):
                for k in range(KD):
                    if k % 2 == 0:
                        act.wait_ge(S["x2_turned"], n * 4 + (k // 2 + 1))
                    ins = A.activation(xT[:, k, :], wide[0][:, (k % 4) * SLOTS:(k % 4 + 1) * SLOTS], ACT.Identity,
                                       scale=scale2[:, k:k + 1], bias=mod2[:, k:k + 1])
                    if k % 2:
                        ins.then_inc(S["x2_made"], 1)

            act.wait_ge(S["tables_ready"], 1)
            for m in range(2):
                A.copy(yT[:, m, 0:1], yT[:, m, 1:2]).then_inc(S["y_copied"], 1)
            turn_x(0)
            with act.Fori(0, VISITS) as v:
                cls = act.value_load(v_int[0:1, 1, bass.ds(v, 1)], min_val=0, max_val=CLASSES)
                with act.If(cls > 0):
                    for j in range(FT):
                        act.wait_ge(S["g_made"], v * FT + (j + 1))
                        A.activation(s_buf[:, j % 2, :], g_buf[:, j % 2, :], ACT.Sigmoid, scale=ALPHA).then_inc(S["s_made"], 1)
                    turn_x(v + 1)
                    for m in range(KD):
                        act.wait_ge(S["y_summed"], v * KD + (m + 1))
                        A.copy(yT[:, m, :], half(6 + m % 2)[:, 0:SLOTS]).then_inc(S["y_copied"], 1)
            for t in range(TT):
                act.wait_ge(fin_loaded[t % 4], 16 * (t // 4 + 1))
                if t >= 1:
                    act.wait_ge(S["fin_ssq"], t)
                A.activation(fin_square, fin[:, t % 4, :], ACT.Square, accum_out=ssq3[:, t:t + 1]).then_inc(S["fin_ssq"], 1)

        @block.vector
        def _(dve):
            link = Chain(dve, S["chain_dve"])
            V = nc.vector
            dve.wait_ge(S["iotas_made"], 2)
            V.tensor_copy(iota_b[:, :], iota_i)
            V.tensor_copy(iota_f[:, :], iota_i[:, 0:NE])
            dve.wait_ge(S["rows_turned"], 1)
            V.tensor_copy(cols[:, :], bank[0][:, 0:84])
            V.tensor_copy(conv_cols[:, :], bank[0][:, P:P + TAPS * CT])
            V.tensor_copy(freq[:, :], bank[0][:, 2 * P:2 * P + 1])
            link(V.tensor_copy(bgu[:, :, :].rearrange("p e j -> p (e j)"), bank[1][:, :]))
            V.tensor_scalar(bgu[:, :, FT:2 * FT], bgu[:, :, FT:2 * FT], 1.0, None, ALU.add).then_inc(S["cols_made"], 1)
            dve.wait_ge(S["c_sigmoid"], 1)
            V.tensor_tensor(c_act[:, :], cols[:, 0:KD], c_sigm[:, :], ALU.mult).then_inc(S["c_ready"], 1)
            dve.wait_ge(S["c_ready"], 1)
            for k in range(KD):
                ins = V.tensor_scalar(c_bc[:, k, :], ones[:, :], c_act[:, k:k + 1], None, ALU.mult)
            ins.then_inc(S["c_spread"], 1)
            dve.wait_ge(S["small_loaded"], 16 * 13)
            link(V.tensor_copy(tmp[1], tmp[0].bitcast(I32)))
            link(V.tensor_scalar(tmp[0], tmp[1], freq[:, 0:1], None, ALU.mult))
            link(V.tensor_scalar(tmp[1], tmp[0], 1.0 / (2 * math.pi), None, ALU.mult))
            link(V.tensor_scalar(tmp[1], tmp[1], ROUND, None, ALU.add))
            link(V.tensor_scalar(tmp[1], tmp[1], -ROUND, None, ALU.add))
            for two_pi in (TWO_PI_A, TWO_PI_B, TWO_PI_C):
                link(V.scalar_tensor_tensor(out=tmp[0], in0=tmp[1], scalar=-two_pi, in1=tmp[0], op0=ALU.mult, op1=ALU.add))
            link(V.tensor_scalar(tmp[1], tmp[0], 3.1415925, -3.1415925, ALU.min, ALU.max))
            link(V.tensor_scalar(tmp[2], tmp[1], -1.0, None, ALU.mult))
            link(V.tensor_tensor(tmp[2], tmp[1], tmp[2], ALU.min))
            V.tensor_scalar(tmp[2], tmp[2], math.pi / 2, None, ALU.add).then_inc(S["angles_made"], 1)
            for t in range(TT):
                dve.wait_ge(S["rstd_made"], t + 1)
                V.tensor_scalar(x_in[:, t, :], x_in[:, t, :], rstd[:, t:t + 1], None, ALU.mult).then_inc(S["x_scaled"], 1)
            dve.wait_ge(S["mod_summed"], 8)
            link(V.tensor_tensor(mod1[:, :], bank[2][:, 0:2 * KD], cols[:, C_ADA:C_ADA + 2 * KD], ALU.add))
            link(V.tensor_scalar(scale1[:, :], mod1[:, KD:2 * KD], 1.0, None, ALU.add))
            V.tensor_tensor(scale1[:, :], scale1[:, :], cols[:, C_MIX:C_MIX + KD], ALU.mult).then_inc(S["scale1_made"], 1)
            dve.wait_ge(S["scale1_made"], 1)
            dve.wait_ge(S["ssq_made"], TT)
            for n in range(1, 2 * KD, 2):
                g, k = n // KD, n % KD
                dve.wait_ge(S["x_turned"], n + 1)
                V.tensor_scalar(hT[:, k, g * HALF:(g + 1) * HALF], half(n % 4), scale1[:, k:k + 1], mod1[:, k:k + 1],
                                ALU.mult, ALU.add).then_inc(S["h_odd"], 1)
            dist = tmp[3].bitcast(I32)
            dve.wait_ge(S["sines_made"], 1)
            link(V.tensor_scalar(tmp[1], dist, 0.0, None, ALU.is_ge))
            link(V.scalar_tensor_tensor(out=mask, in0=dist, scalar=float(P), in1=tmp[1], op0=ALU.is_le, op1=ALU.mult))
            for low, window in ((3, 512), (15, 2048)):
                link(V.tensor_scalar(tmp[0].bitcast(I32), dist, low, None, ALU.bitwise_and))
                link(V.scalar_tensor_tensor(out=tmp[0], in0=tmp[0].bitcast(I32), scalar=0.0, in1=tmp[1], op0=ALU.is_equal, op1=ALU.mult))
                link(V.scalar_tensor_tensor(out=tmp[0], in0=dist, scalar=float(window), in1=tmp[0], op0=ALU.is_le, op1=ALU.mult))
                link(V.tensor_tensor(mask, mask, tmp[0], ALU.add))
            link(V.tensor_scalar(tmp[0], mask, 2.0, 8 * math.log(2.0), ALU.is_ge, ALU.mult))
            link(V.tensor_scalar(tmp[1], mask, 3.0, 8 * math.log(1.5), ALU.is_ge, ALU.mult))
            link(V.tensor_tensor(tmp[0], tmp[0], tmp[1], ALU.add))
            link(V.tensor_scalar(tmp[1], mask, 1.0, -BIG, ALU.is_lt, ALU.mult))
            link(V.tensor_tensor(mask, tmp[0], tmp[1], ALU.add))
            for ct in range(CT):
                ins = V.memset(u_pad[:, ct, 0:TAPS - 1], 0.0)
            link(ins)
            V.memset(top_e[:, 0, 6:8], 0.0).then_inc(S["zeros_made"], 1)
            for ct in range(CT):
                for h in range(2):
                    dve.wait_ge(S["a_copied"], 2 * ct + h + 1)
                    dve.wait_ge(S["sig_made"], 2 * ct + h + 1)
                    uv = u_pad[:, ct, TAPS - 1 + h * HALF:TAPS - 1 + (h + 1) * HALF]
                    V.tensor_tensor(uv, uv, sig_g[:, ct, h * HALF:(h + 1) * HALF], ALU.mult).then_inc(S["u_made"], 1)
                dve.wait_ge(S["u_made"], 2 * ct + 2)
                for w in range(TAPS):
                    src, tap = u_pad[:, ct, w:w + T], conv_cols[:, w * CT + ct:w * CT + ct + 1]
                    if w == 0:
                        link(V.tensor_scalar(conv[:, ct, :], src, tap, cols[:, C_CB + ct:C_CB + ct + 1], ALU.mult, ALU.add))
                        continue
                    ins = V.scalar_tensor_tensor(out=conv[:, ct, :], in0=src, scalar=tap, in1=conv[:, ct, :], op0=ALU.mult, op1=ALU.add)
                    if w < TAPS - 1:
                        link(ins)
                ins.then_inc(S["conv_made"], 1)
            dve.wait_ge(S["conv_made"], CT)
            for i in range(4 * QT):
                dst, f = (qT, i // 2) if i < 2 * QT else (kT, i // 2 - QT)
                hs = slice((i % 2) * HALF, (i % 2 + 1) * HALF)
                dve.wait_ge(S["rot_summed"], i + 1)
                V.tensor_tensor(rot_tmp[i % 2], half(2 + i % 2), sin_t[:, hs], ALU.mult).then_inc(S["rot_read"], 1)
                link(V.tensor_tensor(dst[:, f, hs], dst[:, f, hs], cos_t[:, hs], ALU.mult))
                dve.wait_ge(S["rot_read"], i + 1)
                V.tensor_tensor(dst[:, f, hs], dst[:, f, hs], rot_tmp[i % 2], ALU.add).then_inc(S["q_rotated"], 1)
            for i in range(2 * CT):
                h, ct = i // CT, i % CT
                dve.wait_ge(S["mean_summed"], h + 1)
                yv = conv[:, ct, h * HALF:(h + 1) * HALF]
                V.scalar_tensor_tensor(out=yv, in0=half(4 + h), scalar=-1.0 / CH, in1=yv, op0=ALU.mult, op1=ALU.add).then_inc(S["centred"], 1)
            dve.wait_ge(S["var_summed"], 2 * CT)
            dve.wait_ge(S["q_rotated"], 4 * QT)
            V.tensor_scalar(norm_tmp[1], wide[1][:, :], 1.0 / CH, EPS, ALU.mult, ALU.add).then_inc(S["var_made"], 1)
            dve.wait_ge(S["gates_summed"], 4)
            V.tensor_tensor(gate1_b[:, :], gate1_b[:, :], wide[0][:, :], ALU.add).then_inc(S["gate_made"], 1)
            dve.wait_ge(S["centred"], 2 * CT)
            dve.wait_ge(S["std_made"], 1)
            link(V.reciprocal(norm_tmp[1], norm_tmp[0]))
            for ct in range(CT):
                link(V.tensor_tensor(conv[:, ct, :], conv[:, ct, :], norm_tmp[1], ALU.mult))
                V.tensor_scalar(conv[:, ct, :], conv[:, ct, :], cols[:, C_LG + ct:C_LG + ct + 1], cols[:, C_LB + ct:C_LB + ct + 1],
                                ALU.mult, ALU.add).then_inc(S["z_made"], 1)
            for ct in range(CT):
                dve.wait_ge(S["z_sigmoid"], ct + 1)
                V.tensor_tensor(conv[:, ct, :], conv[:, ct, :], norm_tmp[2 + ct % 2], ALU.mult).then_inc(S["conv_out"], 1)
            dve.wait_ge(S["mod_summed"], 16)
            link(V.tensor_tensor(mod2[:, :], bank[2][:, 0:2 * KD], cols[:, C_ADA + 3 * KD:C_ADA + 5 * KD], ALU.add))
            link(V.tensor_scalar(scale2[:, :], mod2[:, KD:2 * KD], 1.0, None, ALU.add))
            V.tensor_tensor(scale2[:, :], scale2[:, :], cols[:, C_FFN:C_FFN + KD], ALU.mult).then_inc(S["scale2_made"], 1)
            dve.wait_ge(S["gates_summed"], 8)
            dve.wait_ge(S["gate2_loaded"], 16)
            V.tensor_tensor(gate2_b, gate2_b, wide[0][:, :], ALU.add).then_inc(S["gate_made"], 1)

            def copy_turned(i):
                n = (i // HEADS + 1) * P
                if n > HALF:
                    dve.wait_ge(S["prob_turned"], i + 1)
                    dve.wait_ge(S["weighed"], i - 1)
                    V.tensor_copy(probT[i % 2][:, HALF:n], half(1)[:, 0:n - HALF]).then_inc(S["probT_dve"], 1)

            def normalise(i):
                qt, h = i // HEADS, i % HEADS
                dve.wait_ge(S["weighed"], i + 1)
                if qt >= 2 and h == 0:
                    dve.wait_ge(S["attn_turned"], qt - 1)
                link(V.reciprocal(soft[:, i % 4, 3:4], soft[:, i % 4, 2:3]))
                V.tensor_scalar(o_nat[qt % 2][:, h * HD:(h + 1) * HD], half(2 + i % 2)[:, h * HD:(h + 1) * HD], soft[:, i % 4, 3:4], None,
                                ALU.mult).then_inc(S["o_made"], 1)

            ITEMS = TT * HEADS
            for i in range(ITEMS):
                n = (i // HEADS + 1) * P
                dve.wait_ge(S["scored"], i + 1)
                if i >= 2:
                    dve.wait_ge(S["prob_turned"], i - 1)
                link(V.tensor_tensor_reduce(out=prob[i % 2][:, 0:n], in0=wide[i % 2][:, 0:n], in1=mask[:, T - n:T], scale=1.0,
                                            scalar=-3e38, op0=ALU.add, op1=ALU.max, accum_out=soft[:, i % 4, 0:1]))
                V.tensor_scalar(soft[:, i % 4, 1:2], soft[:, i % 4, 0:1], -(HD ** -0.5), None, ALU.mult).then_inc(S["score_masked"], 1)
                if i >= 1:
                    copy_turned(i - 1)
                if i >= 2:
                    normalise(i - 2)
            copy_turned(ITEMS - 1)
            normalise(ITEMS - 2)
            normalise(ITEMS - 1)

            def residual(t):
                b = t % 2
                dve.wait_ge(S["mixed"], t + 1)
                dve.wait_ge(x_back[b], 16 * (t // 2 + 1))
                if t >= 2:
                    dve.wait_ge(S["acc_made"], t - 1)
                V.tensor_tensor(x1[b], wide[0][:, :], gate1_b[:, :], ALU.mult).then_inc(S["mix_read"], 1)
                dve.wait_ge(S["mix_read"], t + 1)
                V.tensor_tensor(x1[b], x1[b], x_again[:, b, :], ALU.add).then_inc(S["x1_made"], 1)
                dve.wait_ge(S["x1_made"], t + 1)
                dve.wait_ge(S["rstd2_made"], t + 1)
                if t == 1:
                    dve.wait_ge(S["scattered_a"], 16)
                    dve.wait_ge(S["scattered_b"], 16)
                if t >= 2:
                    dve.wait_ge(xn_stored[b], 16 * (t // 2))
                V.tensor_scalar(xn1[b], x1[b], rstd2[:, t:t + 1], None, ALU.mult).then_inc(S["xn_made"], 1)

            def route(t):
                b = t % 2
                dve.wait_ge(S["xn_turned"], t + 1)
                for k in range(KD // 2, KD):
                    ins = V.tensor_scalar(h2T[b][:, k, :], wide[1][:, k * P:(k + 1) * P], scale2[:, k:k + 1], mod2[:, k:k + 1],
                                          ALU.mult, ALU.add)
                ins.then_inc(S["h2_high"], 1)
                dve.wait_ge(S["logits_summed"], t + 1)
                link(V.tensor_tensor(logit[:, :], bank[3][:, 0:NE], br[:, :], ALU.add))
                link(V.max(out=top[:, b, :], in_=logit[:, :]))
                V.tensor_scalar(top_e[:, b, 4:5], top[:, b, 0:1], -1.0, None, ALU.mult).then_inc(S["top_made"], 1)
                link(V.max_index(out=top_i[:, :], in_max=top[:, b, :], in_values=logit[:, :]))
                link(V.tensor_copy(top_f[:, :], top_i[:, :]))
                dve.wait_ge(S["exp4_made"], t + 1)
                link(V.reciprocal(top_e[:, b, 6:7], top_e[:, b, 5:6]))
                link(V.tensor_scalar(gate4[:, :], top_e[:, b, 0:TOPK], top_e[:, b, 6:7], None, ALU.mult))
                for k in range(TOPK):
                    link(V.tensor_scalar(hit[:, :], iota_f[:, :], top_f[:, k:k + 1], None, ALU.is_equal))
                    if k == 0:
                        link(V.tensor_scalar(gates[:, t, :], hit[:, :], gate4[:, 0:1], None, ALU.mult))
                        link(V.tensor_copy(picked[:, b, :], hit[:, :]))
                    else:
                        link(V.scalar_tensor_tensor(out=gates[:, t, :], in0=hit[:, :], scalar=gate4[:, k:k + 1], in1=gates[:, t, :],
                                                    op0=ALU.mult, op1=ALU.add))
                        link(V.tensor_tensor(picked[:, b, :], picked[:, b, :], hit[:, :], ALU.add))
                V.tensor_copy(picked_b[:, b, :], picked[:, b, :])
                V.tensor_copy(so_far_b[:, b, :], so_far[:, :]).then_inc(S["picked_made"], 1)
                link(V.tensor_tensor(so_far[:, :], so_far[:, :], picked[:, b, :], ALU.add))

            def enlist(t):
                b = t % 2
                dve.wait_ge(S["placed"], t + 1)
                V.tensor_copy(gatesT[:, :], bank[3][0:NE, P:2 * P]).then_inc(S["gatesT_made"], 1)
                link(V.scalar_tensor_tensor(out=place[:, t, :], in0=bank[3][:, 2 * P:2 * P + NE], scalar=-NEVER, in1=picked[:, b, :],
                                            op0=ALU.add, op1=ALU.mult))
                link(V.tensor_scalar(place[:, t, :], place[:, t, :], NEVER, None, ALU.add))
                dve.wait_ge(S["bd_summed"], 2 * t + 2)
                if t >= 2:
                    dve.wait_ge(acc_stored[b], 16 * (t // 2))
                for h in range(2):
                    hs = slice(h * HALF, (h + 1) * HALF)
                    V.tensor_tensor(acc_sb[b][:, hs], half(1 + h), gate2_b[:, hs], ALU.mult).then_inc(S["bd_read"], 1)
                dve.wait_ge(S["bd_read"], 2 * t + 2)
                V.tensor_tensor(acc_sb[b], acc_sb[b], x1[b], ALU.add).then_inc(S["acc_made"], 1)

            dve.wait_ge(S["o_made"], ITEMS)
            dve.wait_ge(S["weighed"], ITEMS)
            V.memset(xn1[1], 0.0).then_inc(S["zeros_made"], 1)
            link(V.memset(so_far[:, :], 0.0))
            for t in range(TT + 2):
                if t >= 2:
                    enlist(t - 2)
                if t < TT:
                    residual(t)
                if 1 <= t <= TT:
                    route(t - 1)

            V.tensor_copy(so_far_b[:, 0, :], so_far[:, :]).then_inc(S["picked_made"], 1)
            dve.wait_ge(S["counted"], 1)
            link(V.tensor_copy(cnt[:, :], bank[3][:, 3 * P:3 * P + NE]))
            link(V.tensor_scalar(v_tab[:, 1, 0:NE], cnt[:, :], 64.0, 1.0, ALU.is_gt, ALU.add))
            for q in (128.0, 192.0):
                link(V.scalar_tensor_tensor(out=v_tab[:, 1, 0:NE], in0=cnt[:, :], scalar=q, in1=v_tab[:, 1, 0:NE], op0=ALU.is_gt, op1=ALU.add))
            link(V.tensor_scalar(more_e[:, :], cnt[:, :], float(SLOTS), None, ALU.is_gt))
            for q in (2.0 * SLOTS, 3.0 * SLOTS):
                link(V.scalar_tensor_tensor(out=more_e[:, :], in0=cnt[:, :], scalar=q, in1=more_e[:, :], op0=ALU.is_gt, op1=ALU.add))
            link(V.memset(hit[:, :], 0.0))
            link(V.tensor_tensor_scan(out=incl[:, :], data0=more_e[:, :], data1=hit[:, :], initial=0.0, op0=ALU.add, op1=ALU.add))
            for o in range(MORE):
                V.tensor_scalar(is_before[:, o, :], incl[:, :], float(o), None, ALU.is_le)
                ins = V.scalar_tensor_tensor(out=more_before[:, o, :], in0=incl[:, :], scalar=float(o), in1=more_e[:, :],
                                             op0=ALU.is_le, op1=ALU.mult)
            link(ins)
            V.reduce_sum(out=o_tmp[:, 0, :], in_=is_before, axis=AX_X)
            V.reduce_sum(out=o_tmp[:, 1, :], in_=more_before, axis=AX_X)
            link(V.tensor_scalar(o_tmp[:, 2, :], iota_f[:, 0:MORE], incl[:, NE - 1:NE], None, ALU.is_lt))
            link(V.tensor_tensor(v_tab[:, 0, NE:VISITS], o_tmp[:, 0, :], o_tmp[:, 2, :], ALU.mult))
            link(V.tensor_scalar(v_tab[:, 1, NE:VISITS], o_tmp[:, 2, :], float(CLASSES), None, ALU.mult))
            link(V.tensor_tensor(o_tmp[:, 3, :], iota_f[:, 0:MORE], o_tmp[:, 1, :], ALU.subtract))
            link(V.tensor_scalar(o_tmp[:, 3, :], o_tmp[:, 3, :], float(SLOTS), float(SLOTS) - NEVER, ALU.mult, ALU.add))
            link(V.tensor_tensor(o_tmp[:, 3, :], o_tmp[:, 3, :], o_tmp[:, 2, :], ALU.mult))
            link(V.tensor_scalar(v_tab[:, 2, NE:VISITS], o_tmp[:, 3, :], NEVER, None, ALU.add))
            link(V.tensor_copy(v_tab[:, 0, 0:NE], iota_f[:, :]))
            link(V.tensor_copy(v_int[:, :, :], v_tab[:, 0:2, :]))
            link(V.tensor_scalar(n_vis[:, :], incl[:, NE - 1:NE], float(NE), None, ALU.add))
            link(V.tensor_copy(g_cols[:, :, :, 3], gates))
            link(V.tensor_tensor(g_rest, gates, g_cols[:, :, :, 3], ALU.subtract))
            link(V.tensor_copy(g_cols[:, :, :, 4], g_rest))
            link(V.tensor_tensor(g_rest, g_rest, g_cols[:, :, :, 4], ALU.subtract))
            link(V.tensor_copy(g_cols[:, :, :, 5], g_rest))
            for b in range(2):
                dve.wait_ge(acc_stored[b], 16 * TT // 2)
            for buf in (got[0], got[1], part(at_y, 4 * D)):
                V.memset(buf, 0.0)
            V.tensor_copy(here[:, 0, :], slot_id[:, :])
            link(V.memset(wide[1][:, :], 0.0))
            for ps in bank:
                V.memset(ps[:, :], 0.0).then_inc(S["pair_read"], 1)
            dve.wait_ge(S["pair_read"], 4)
            V.memset(o_tmp[:, 3, :], 0.0).then_inc(S["tables_ready"], 1)

            def write_list(n):
                e = dve.value_load(v_int[0:1, 0, bass.ds(n, 1)], min_val=0, max_val=NE - 1)
                V.tensor_copy(g_e[:, :, :], g_cols[:, :, bass.ds(e, 1), :].rearrange("p t a n -> p t (a n)"))
                link(V.tensor_scalar(place_e[:, :], place[:, :, bass.ds(e, 1)].rearrange("p t a -> p (t a)"),
                                     v_tab[:, 2, bass.ds(n, 1)], None, ALU.subtract))
                for t in range(TT):
                    ins = V.tensor_scalar(onehot[:, t, :], iota_b[:, :], place_e[:, t:t + 1], None, ALU.is_equal)
                ins.then_inc(S["list_made"], 1)

            def read_list(n):
                dve.wait_ge(S["list_summed"], n + 1)
                link(V.tensor_copy(list_sb[:, :, :], list_ps))
                V.tensor_tensor(look[:, 0, :], list_sb[:, :, 0], list_sb[:, :, 1], ALU.add)
                V.tensor_tensor(list_sb[:, :, 6], slot_id[:, :], list_sb[:, :, 2], ALU.mult)
                link(V.tensor_tensor(look[:, 1, :], list_sb[:, :, 3], list_sb[:, :, 4], ALU.add))
                V.tensor_tensor(list_sb[:, :, 7], slot_id[:, :], list_sb[:, :, 6], ALU.subtract)
                link(V.tensor_tensor(look[:, 1, :], look[:, 1, :], list_sb[:, :, 5], ALU.add))
                link(V.tensor_tensor(look[:, 0, :], look[:, 0, :], list_sb[:, :, 7], ALU.add))
                V.tensor_copy(gather_i[:, :], look[:, 0, :]).then_inc(S["gather_ready"], 1)

            def shift_lists(v):
                dve.wait_ge(S["scattered_a"], v * 16 + 16)
                dve.wait_ge(S["scattered_b"], v * 16 + 16)
                V.tensor_copy(scatter_i[:, :], here[:, 0, :])
                link(V.tensor_copy(gone_g[:, :], here[:, 1, :]))

            def y_out(n):
                for i in range(4):
                    b, h = i // 2, i % 2
                    dve.wait_ge(S["y_turned"], n * 4 + (i + 1))
                    hs = slice(h * HALF, (h + 1) * HALF)
                    V.scalar_tensor_tensor(out=y_nat[b][:, hs], in0=half(4 + h), scalar=gone_g[:, b:b + 1], in1=gate2_b[:, hs],
                                           op0=ALU.mult, op1=ALU.mult).then_inc(S["y_made"], 1)

            def finish_pair(v, j):
                dve.wait_ge(S["s_made"], v * FT + (j + 1))
                dve.wait_ge(S["t_made"], v * FT + (j + 1))
                V.tensor_tensor(actT[:, j, :], t_buf[:, j % 2, :], s_buf[:, j % 2, :], ALU.mult).then_inc(S["act_made"], 1)

            write_list(0)
            read_list(0)
            with dve.Fori(0, VISITS) as v:
                cls = dve.value_load(v_int[0:1, 1, bass.ds(v, 1)], min_val=0, max_val=CLASSES)
                with dve.If(cls > 0):
                    link.loop(v, LINKS_PER_VISIT)
                    e = dve.value_load(v_int[0:1, 0, bass.ds(v, 1)], min_val=0, max_val=NE - 1)
                    shift_lists(v)
                    V.tensor_copy(here[:, :, :], look[:, :, :])
                    link(V.tensor_copy(bias_e[:, :], bgu[:, bass.ds(e, 1), :].rearrange("p a j -> p (a j)")))
                    write_list(v + 1)
                    for j in range(FT):
                        if j == 2:
                            y_out(v)
                        if j == 4:
                            read_list(v + 1)
                        ps = bank[j % 4]
                        dve.wait_ge(S["pair_summed"], v * FT + (j + 1))
                        V.tensor_scalar(g_buf[:, j % 2, :], ps[:, 0:SLOTS], bias_e[:, j:j + 1], LIMIT, ALU.add,
                                        ALU.min).then_inc(S["g_made"], 1)
                        V.tensor_scalar(u_buf[:, j % 2, :], ps[:, SLOTS:2 * SLOTS], bias_e[:, FT + j:FT + j + 1], LIMIT + 1,
                                        ALU.add, ALU.min).then_inc(S["pair_read"], 1)
                        if j >= 1:
                            finish_pair(v, j - 1)
                        dve.wait_ge(S["pair_read"], v * FT + (j + 5))
                        V.scalar_tensor_tensor(out=t_buf[:, j % 2, :], in0=u_buf[:, j % 2, :], scalar=1.0 - LIMIT, in1=g_buf[:, j % 2, :],
                                               op0=ALU.max, op1=ALU.mult).then_inc(S["t_made"], 1)
                    finish_pair(v, FT - 1)
            n = dve.value_load(n_vis[0:1, 0:1], min_val=NE, max_val=VISITS)
            link.end(n)
            shift_lists(n)
            y_out(n)
            dve.wait_ge(S["g_final_loaded"], 16)
            for t in range(TT):
                dve.wait_ge(S["fin_rstd"], t + 1)
                V.scalar_tensor_tensor(out=fin[:, t % 4, :], in0=fin[:, t % 4, :], scalar=rstd3[:, t:t + 1], in1=g_fin_b,
                                       op0=ALU.mult, op1=ALU.mult).then_inc(S["fin_made"], 1)

        @block.tensor
        def _(pe):
            M = nc.tensor

            def piece(n):
                pe.wait_ge(dense_loaded[n % RING1], 16 * (n // RING1 + 1))
                return dense_piece(n)

            def product(ps, pairs):
                pairs = list(pairs)
                for i, (w, m) in enumerate(pairs):
                    ins = M.matmul(ps, w, m, start=i == 0, stop=i == len(pairs) - 1)
                return ins

            pe.wait_ge(S["idents_made"], 1)
            pe.wait_ge(S["small_loaded"], 16 * 13)
            M.transpose(bank[0][:, 0:84], row_a[0:84, :], ident[0:84, 0:84])
            M.transpose(bank[0][:, P:P + TAPS * CT], row_c[0:TAPS * CT, :], ident[0:TAPS * CT, 0:TAPS * CT])
            M.transpose(bank[0][:, 2 * P:2 * P + 1], freq_row[0:1, :], ident[0:1, 0:1])
            for q in range(4):
                ins = M.transpose(bank[1][:, q * P:(q + 1) * P], row_g[:, q, :], ident[:, :])
            ins.then_inc(S["rows_turned"], 1)

            def mod_columns(first, at):
                for i in range(8):
                    w = piece(first + i)
                    for j in range(2):
                        col = 2 * i + j
                        ins = product(bank[2][:, col:col + 1], ((w[:, k, j * P:(j + 1) * P], c_act[:, k:k + 1]) for k in range(KD)))
                    ins.then_inc(S["mod_summed"], 1)

            def mod_rows(first):
                for i in range(4):
                    w = piece(first + i)
                    product(wide[0][:, i * PIECE:(i + 1) * PIECE], ((c_bc[:, k, :], w[:, k, :]) for k in range(KD))).then_inc(S["gates_summed"], 1)

            pe.wait_ge(S["c_ready"], 1)
            mod_columns(0, 0)
            for n in range(2 * KD):
                g, k = n // KD, n % KD
                pe.wait_ge(S["x_scaled"], 4 * (g + 1))
                if n < 4:
                    pe.wait_ge(S["scale1_made"], 1)
                else:
                    pe.wait_ge(S["h_even" if n % 2 == 0 else "h_odd"], n // 2 - 1)
                for j in range(4):
                    ins = M.transpose(half(n % 4)[:, j * P:(j + 1) * P], x_in[:, 4 * g + j, k * P:(k + 1) * P], ident[:, :])
                ins.then_inc(S["x_turned"], 1)
            pe.wait_ge(S["h_even"], KD)
            pe.wait_ge(S["h_odd"], KD)
            for i in range(2 * CT):
                ct, h = i // 2, i % 2
                for j in range(2):
                    w = piece(AG + 2 * (ct // 2) + j)
                    if i >= 2:
                        pe.wait_ge(S["sig_made" if j else "a_copied"], i - 1)
                    if i == 0:
                        pe.wait_ge(S["zeros_made"], 1)
                    product(half(4 + (2 * i + j) % 4), ((w[:, k, (ct % 2) * P:(ct % 2 + 1) * P], hT[:, k, h * HALF:(h + 1) * HALF])
                                                        for k in range(KD))).then_inc(S["ag_summed"], 1)
            for i in range(4 * QT):
                f, h = i // 2, i % 2
                w = piece(QK + f // 2)
                if i >= 2:
                    pe.wait_ge(S["qkv_copied"], i - 1)
                product(half(i % 2), ((w[:, k, (f % 2) * P:(f % 2 + 1) * P], hT[:, k, h * HALF:(h + 1) * HALF])
                                      for k in range(KD))).then_inc(S["qkv_summed"], 1)
            for t in range(TT):
                pe.wait_ge(S["qkv_copied"], 4 * QT + t - 1)
                for j in range(2):
                    w = piece(QK + 4 + j)
                    ins = product(half(t % 2)[:, j * PIECE:(j + 1) * PIECE], ((hT[:, k, t * P:(t + 1) * P], w[:, k, :]) for k in range(KD)))
                ins.then_inc(S["qkv_summed"], 1)
                for i in (2 * t, 2 * t + 1):
                    src, f = (qT, i // 2) if i < 2 * QT else (kT, i // 2 - QT)
                    pe.wait_ge(S["qkv_copied"], i + 1)
                    if i >= 2:
                        pe.wait_ge(S["rot_read"], i - 1)
                    M.matmul(half(2 + i % 2), rot_m[:, :], src[:, f, (i % 2) * HALF:(i % 2 + 1) * HALF], start=True,
                             stop=True).then_inc(S["rot_summed"], 1)
            pe.wait_ge(S["conv_made"], CT)
            pe.wait_ge(S["sig_made"], 2 * CT)
            for h in range(2):
                product(half(4 + h), ((ones[:, :], conv[:, ct, h * HALF:(h + 1) * HALF]) for ct in range(CT))).then_inc(S["mean_summed"], 1)
            for i in range(2 * CT):
                h, ct = i // CT, i % CT
                pe.wait_ge(S["squared"], i + 1)
                M.matmul(half(6 + h), ones[:, :], norm_tmp[2 + i % 2][:, 0:HALF], start=ct == 0, stop=ct == CT - 1).then_inc(S["var_summed"], 1)
            pe.wait_ge(S["c_spread"], 1)
            pe.wait_ge(S["centred"], 2 * CT)
            mod_rows(ADA2)
            pe.wait_ge(S["q_rotated"], 4 * QT)
            mod_columns(ADA2 + 4, 0)
            pe.wait_ge(S["gate_made"], 1)
            mod_rows(ADA2 + 12)

            ITEMS = TT * HEADS

            def score(i):
                qt, h = i // HEADS, i % HEADS
                n, rows_h = (qt + 1) * P, slice((h % 2) * HD, (h % 2 + 1) * HD)
                if i >= 2:
                    pe.wait_ge(S["score_masked"], i - 1)
                for at in range(0, n, HALF):
                    m = min(HALF, n - at)
                    ins = M.matmul(wide[i % 2][:, at:at + m], qT[rows_h, h // 2, qt * P:(qt + 1) * P], kT[rows_h, h // 2, at:at + m],
                                   start=True, stop=True)
                ins.then_inc(S["scored"], 1)

            def turn(i):
                pe.wait_ge(S["exped"], i + 1)
                if i >= 1:
                    pe.wait_ge(S["probT_act"], i)
                    if i - 1 >= 4 * HEADS:
                        pe.wait_ge(S["probT_dve"], i - 4 * HEADS)
                for kt in range(i // HEADS + 1):
                    ins = M.transpose(half(kt // 4)[:, (kt % 4) * P:(kt % 4 + 1) * P], prob[i % 2][:, kt * P:(kt + 1) * P], ident[:, :])
                ins.then_inc(S["prob_turned"], 1)

            def weigh(i):
                qt, h = i // HEADS, i % HEADS
                pe.wait_ge(S["probT_act"], i + 1)
                if qt >= 4:
                    pe.wait_ge(S["probT_dve"], i - 4 * HEADS + 1)
                if i >= 2:
                    pe.wait_ge(S["o_made"], i - 1)
                if h == 3 and qt >= 1:
                    turn_attn(qt - 1, i - 1)
                    pe.wait_ge(S["attn_made"], qt)
                product(half(2 + i % 2)[:, h * HD:(h + 1) * HD], ((probT[i % 2][:, kt * P:(kt + 1) * P], v_nat[:, kt, h * HD:(h + 1) * HD])
                                                          for kt in range(qt + 1))).then_inc(S["weighed"], 1)

            def turn_attn(qt, made):
                pe.wait_ge(S["o_made"], made)
                for f in range(QT):
                    ins = M.transpose(half(3)[:, f * P:(f + 1) * P], o_nat[qt % 2][:, f * P:(f + 1) * P], ident[:, :])
                ins.then_inc(S["attn_turned"], 1)

            pe.wait_ge(S["scale2_made"], 1)
            pe.wait_ge(S["gate_made"], 2)
            pe.wait_ge(S["qkv_copied"], 4 * QT + TT)
            score(0)
            score(1)
            for i in range(ITEMS):
                turn(i)
                if i + 2 < ITEMS:
                    score(i + 2)
                weigh(i)
            turn_attn(TT - 1, ITEMS)

            mixT = [conv[:, ct, :] for ct in range(CT)] + [attnT[:, f, :] for f in range(QT)]
            pe.wait_ge(S["conv_out"], CT)
            pe.wait_ge(S["attn_made"], TT)
            pe.wait_ge(S["b_down_loaded"], 16)
            pe.wait_ge(S["consts_made"], 2)
            for t in range(TT + 2):
                if t >= 2:
                    s = t - 2
                    b = s % 2
                    pe.wait_ge(S["picked_made"], s + 1)
                    M.transpose(bank[3][0:NE, P:2 * P], gates[:, s, :], ident[:, :])
                    product(bank[3][:, 2 * P:2 * P + NE], ((before_m[:, :], picked_b[:, b, :]), (ones_b[:, :], so_far_b[:, b, :]))).then_inc(S["placed"], 1)
                    pe.wait_ge(S["gatesT_made"], s + 1)
                    if s >= 1:
                        pe.wait_ge(S["bd_read"], 2 * s)
                    for h in range(2):
                        M.matmul(half(1 + h), gatesT[:, :], b_down_sb[:, h * HALF:(h + 1) * HALF], start=True, stop=True).then_inc(S["bd_summed"], 1)
                if t < TT:
                    if t >= 1:
                        pe.wait_ge(S["mix_read"], t)
                    for i in range(4):
                        w = piece(OUT + i)
                        ins = product(wide[0][:, i * PIECE:(i + 1) * PIECE], ((mixT[k][:, t * P:(t + 1) * P], w[:, k, :]) for k in range(KD)))
                    ins.then_inc(S["mixed"], 1)
                if 1 <= t <= TT:
                    s = t - 1
                    b = s % 2
                    pe.wait_ge(S["xn_made"], s + 1)
                    if s >= 1:
                        pe.wait_ge(S["h2_low"], s)
                        pe.wait_ge(S["h2_high"], s)
                    for k in range(KD):
                        ins = M.transpose(wide[1][:, k * P:(k + 1) * P], xn1[b][:, k * P:(k + 1) * P], ident[:, :])
                    ins.then_inc(S["xn_turned"], 1)
                    pe.wait_ge(S["h2_low"], s + 1)
                    pe.wait_ge(S["h2_high"], s + 1)
                    if s >= 1:
                        pe.wait_ge(S["bd_read"], 2 * s)
                    product(bank[3][:, 0:NE], ((h2T[b][:, k, :], wr[:, k, :]) for k in range(KD))).then_inc(S["logits_summed"], 1)
            pe.wait_ge(S["picked_made"], TT + 1)
            M.matmul(bank[3][:, 3 * P:3 * P + NE], ones_b[:, :], so_far_b[:, 0, :], start=True, stop=True).then_inc(S["counted"], 1)

            def make_list(n):
                pe.wait_ge(S["list_made"], n + 1)
                for b in range(2):
                    ins = product(list_ps[:, b, :], ((onehot[:, t, b * P:(b + 1) * P], g_e[:, t, :]) for t in range(TT)))
                ins.then_inc(S["list_summed"], 1)

            def turn_x(n, first):
                pe.wait_ge(S["gathered_a"], n * 16 + 16)
                pe.wait_ge(S["gathered_b"], n * 16 + 16)
                for q in range(4):
                    if q >= 2:
                        pe.wait_ge(S["x2_made"], n * 4 + (q - 1))
                    elif not first:
                        pe.wait_ge(S["y_made"], n * 4 + (q - 1))
                    for k in (2 * q, 2 * q + 1):
                        for b in range(2):
                            at = (k % 4) * SLOTS + b * P
                            ins = M.transpose(wide[0][:, at:at + P], got[b][:, k * P:(k + 1) * P], ident[:, :])
                    ins.then_inc(S["x2_turned"], 1)

            def turn_y(n):
                pe.wait_ge(S["y_copied"], n * KD + 2)
                pe.wait_ge(S["x2_made"], n * 4 + 4)
                for i in range(4):
                    b, h = i // 2, i % 2
                    if i >= 2:
                        pe.wait_ge(S["y_made"], n * 4 + (i - 1))
                    for m in range(4):
                        ins = M.transpose(half(4 + h)[:, m * P:(m + 1) * P], yT[:, 4 * h + m, b * P:(b + 1) * P], ident[:, :])
                    ins.then_inc(S["y_turned"], 1)

            def visit(v, n):
                for j in range(FT):
                    if j == 0:
                        pe.wait_ge(S["x2_made"], v * 4 + 4)
                    if j == 2:
                        turn_y(v)
                    if j == 4:
                        make_list(v + 1)
                    if j % 2 == 0:
                        pe.wait_ge(piece_loaded[j], v * 16 + 16)
                        pe.wait_ge(piece_loaded[j + 1], v * 16 + 16)
                    pe.wait_ge(S["pair_read"], v * FT + (j + 1))
                    for half_p in range(2):
                        w = ring[:, ring_slot(2 * (j // 2) + half_p)]
                        ins = product(bank[j % 4][:, half_p * SLOTS:half_p * SLOTS + n],
                                      ((w[:, k, (j % 2) * P:(j % 2 + 1) * P], xT[:, k, 0:n]) for k in range(KD)))
                    ins.then_inc(S["pair_summed"], 1)
                turn_x(v + 1, False)
                pe.wait_ge(S["act_made"], v * FT + FT)
                for m in range(KD):
                    if m % 2 == 0:
                        pe.wait_ge(piece_loaded[8 + m // 2], v * 16 + 16)
                    pe.wait_ge(S["y_copied"], v * KD + (m + 1))
                    if m == 1:
                        pe.wait_ge(S["gather_ready"], v + 2)
                    w = ring[:, ring_slot(8 + m // 2)]
                    product(half(6 + m % 2)[:, 0:n],
                            ((w[:, k, (m % 2) * P:(m % 2 + 1) * P], actT[:, k, 0:n]) for k in range(FT))).then_inc(S["y_summed"], 1)

            pe.wait_ge(S["tables_ready"], 1)
            make_list(0)
            turn_x(0, True)
            with pe.Fori(0, VISITS) as v:
                cls = pe.value_load(v_int[0:1, 1, bass.ds(v, 1)], min_val=0, max_val=CLASSES)
                for q in range(1, CLASSES + 1):
                    with pe.If(cls == q):
                        visit(v, q * 64)
            n = pe.value_load(n_vis[0:1, 0:1], min_val=NE, max_val=VISITS)
            turn_y(n)


_IN = ("x", "c", "positions", "w_ada", "b_ada", "g_mix", "w_in", "conv_w", "conv_b", "conv_ln_g", "conv_ln_b", "w_out", "g_ffn",
       "w_router", "b_router", "w_gu", "b_gu", "w_down", "b_down", "g_final")
_SHAPES = {"x": (T, D), "w_ada": (D, 6 * D), "w_in": (D, 2 * CH + 3 * HEADS * HD), "w_out": (D, D), "w_router": (D, NE),
           "w_gu": (NE, D, 2 * D), "w_down": (NE, D, D), "b_down": (NE, D)}


def kernel(**inputs):
    import concourse.bacc as bacc
    from concourse.bass_utils import run_bass_kernel_spmd

    nc = bacc.Bacc("TRN2", target_bir_lowering=False, num_devices=1)
    arrays, views = {}, []
    for name in _IN:
        a = np.asarray(inputs[name])
        a = np.ascontiguousarray(a.reshape(_SHAPES.get(name, (-1,))))
        arrays[f"in_{name}"] = a
        views.append(nc.dram_tensor(f"in_{name}", a.shape, mybir.dt.from_np(a.dtype), kind="ExternalInput").ap())
    out = nc.dram_tensor("out", (T, D), F32, kind="ExternalOutput").ap()
    decoder_layer(nc, *views, out)
    result = run_bass_kernel_spmd(nc, [arrays], core_ids=[0])
    return result.results[0]["out"].reshape(1, T, D)
```

```python
import math
from contextlib import ExitStack

import numpy as np

import concourse.bass as bass
from concourse import mybir

F32 = mybir.dt.float32
BF16 = mybir.dt.bfloat16
I32 = mybir.dt.int32
U32 = mybir.dt.uint32
ALU = mybir.AluOpType
ACT = mybir.ActivationFunctionType
AX_X = mybir.AxisListType.X

P = 128
T = 1024
TT = T // P
D = 1024
KD = D // P
HALF = 512
CH = 512
CT = CH // P
TAPS = 31
PADDED = T + TAPS - 1
HEADS = 8
HD = 64
ROT = 16
THETA = 500000.0
QT = HEADS * HD // P
NE = 32
TOPK = 4
LIMIT = 7.0
ALPHA = 1.702
EPS = 1e-6
PIECE = 256
SLOTS = 256
WIDTHS = tuple(range(64, SLOTS + 1, 16))
CLASSES = len(WIDTHS)
MORE = 16
VISITS = NE + MORE
GROUP = 16
NEVER = 8192.0
RING = 12
RING1 = 8
BIG = 1e30
FT = D // P
FEW_CLASSES = WIDTHS.index(P) + 1
LINKS_PER_VISIT = 7
ROUND = 12582912.0
TWO_PI_A = 6.28125
TWO_PI_B = float(np.float32(round((2 * math.pi - 6.28125) * 2**20) / 2**20))
TWO_PI_C = float(2 * math.pi - TWO_PI_A - TWO_PI_B)


class Chain:

    def __init__(self, engine, sem):
        self.engine, self.sem, self.count, self.base = engine, sem, 0, 0

    def loop(self, turn, per):
        self.start, self.per = self.count, per
        self.base = turn * per

    def end(self, times):
        assert self.count - self.start == self.per, (self.count - self.start, self.per)
        self.base = (times - 1) * self.per

    def __call__(self, ins):
        self.count += 1
        ins.then_inc(self.sem, 1)
        self.engine.wait_ge(self.sem, self.base + self.count)


def decoder_layer(nc, x, c, positions, w_ada, b_ada, g_mix, w_in, conv_w, conv_b, conv_ln_g, conv_ln_b,
                  w_out, g_ffn, w_router, b_router, w_gu, b_gu, w_down, b_down, g_final, out):
    ctx = ExitStack()
    with ctx:
        def sb(name, shape, dt=F32):
            return ctx.enter_context(nc.sbuf_tensor(name, shape, dt))

        def sem(name):
            return ctx.enter_context(nc.semaphore(name))

        xn_rows = nc.dram_tensor("xn_rows", (T, D), F32).ap()
        sum_rows = nc.dram_tensor("sum_rows", (T + SLOTS, D), F32).ap()

        ring = sb("ring", [P, RING, KD, PIECE])
        high = ring[:, RING1:RING].rearrange("p s k n -> p (s k n)")
        qT = high[:, 0:QT * T].rearrange("p (f t) -> p f t", f=QT)
        kT = high[:, QT * T:2 * QT * T].rearrange("p (f t) -> p f t", f=QT)

        at_h = 0
        at_u = at_h + KD * T
        at_y = at_u + CT * PADDED
        at_v = at_y + CT * T
        at_trig = at_v + TT * HALF
        at_mask = at_trig + 2 * T
        arena = sb("arena", [P, at_mask + T])

        def part(start, size, **dims):
            view = arena[:, start:start + size]
            if dims:
                (name, n), = dims.items()
                view = view.rearrange(f"p ({name} n) -> p {name} n", **{name: n})
            return view

        hT = part(at_h, KD * T, k=KD)
        row_a, row_c, freq_row = (part(at_h + 4096 + i * P, P) for i in range(3))
        row_g = part(at_h + 4608, 4 * P, q=4)
        iota_i = part(at_h + 5120, SLOTS).bitcast(I32)
        mod_row = part(at_h + 6144, 2 * D)[0:1, :]
        u_pad = part(at_u, CT * PADDED, c=CT)
        conv = part(at_y, CT * T, c=CT)
        x_in = part(at_y, TT * D, t=TT)
        sig_g = part(at_v, CT * T, c=CT)
        v_nat = part(at_v, TT * HALF, t=TT)
        cos_t, sin_t = part(at_trig, T), part(at_trig + T, T)
        mask = part(at_mask, T)
        tmp = [part(at_u + i * T, T) for i in range(4)]
        rot_tmp = [part(at_u + i * HALF, HALF) for i in range(2)]
        norm_tmp = [part(at_u + i * T, T) for i in range(4)]
        attnT = part(at_h, QT * T, f=QT)
        prob = [part(at_h + 4096 + i * T, T) for i in range(2)]
        probT = [part(at_h + 6144 + i * T, T) for i in range(2)]
        o_nat = [part(at_trig + i * HALF, HALF) for i in range(2)]
        x_again = part(at_u, 2 * D, t=2)
        x1 = [part(at_h + 4096 + i * D, D) for i in range(3)]
        xn1 = part(at_h + 7168, D)
        h2T = [part(at_v + i * D, D, k=KD) for i in range(2)]
        acc_sb = [part(at_v + 2 * D + i * D, D) for i in range(2)]
        square = part(at_trig, D)
        b_down_sb = arena[0:NE, at_trig + D:at_trig + 2 * D]
        gate2_b = part(at_u + 2 * D, D)
        g_cols = part(at_u + 3 * D, TT * NE * 4).bitcast(BF16).rearrange("p (t e n) -> p t e n", t=TT, e=NE)
        gates = part(at_mask, TT * NE, t=TT)
        place = part(at_mask + TT * NE, TT * NE, t=TT)
        g_rest = part(at_mask + 2 * TT * NE, TT * NE, t=TT)
        is_before = part(at_y, MORE * NE, o=MORE)
        more_before = part(at_y + MORE * NE, MORE * NE, o=MORE)
        o_tmp = part(at_y + 2 * MORE * NE, 4 * MORE, q=4)
        xT = part(at_v, KD * SLOTS, k=KD)
        got = [part(at_v + 2 * D + b * D, D) for b in range(2)]
        actT = part(at_y, FT * SLOTS, k=FT)
        yT = part(at_y + FT * SLOTS, KD * SLOTS, k=KD)
        y_nat = [part(at_h + b * D, D) for b in range(2)]
        onehot = part(at_h + 2 * D, TT * SLOTS // 2).bitcast(BF16).rearrange("p (t n) -> p t n", t=TT)
        g_buf, u_buf, s_buf, t_buf = (part(at_h + 3 * D + i * 2 * SLOTS, 2 * SLOTS, k=2) for i in range(4))
        fin = ring[:, 0:4].rearrange("p s k n -> p (s k n)").rearrange("p (t n) -> p t n", t=TT)
        fin_square = part(at_y, 2 * D, t=2)
        g_fin_b = part(at_trig, D)

        ident = sb("ident", [P, P])
        ones = sb("ones", [P, P])
        rot_m = sb("rot_m", [P, P])
        before_m = sb("before_m", [P, P], BF16)
        ones_b = sb("ones_b", [P, P], BF16)
        cols = sb("cols", [P, 84])
        C_ADA, C_MIX, C_FFN, C_CB, C_LG, C_LB = 8, 56, 64, 72, 76, 80
        conv_cols = sb("conv_cols", [P, TAPS * CT])
        bgu = sb("bgu", [P, NE, 2 * FT])
        c_sigm = sb("c_sigm", [P, KD])
        c_act = sb("c_act", [P, KD])
        c_bc = sb("c_bc", [P, KD, P])
        mod1 = sb("mod1", [P, 2 * KD])
        mod2 = sb("mod2", [P, 2 * KD])
        scale1 = sb("scale1", [P, KD])
        scale2 = sb("scale2", [P, KD])
        gate1_b = sb("gate1_b", [P, D])
        freq = sb("freq", [P, 1])
        settled = sb("settled", [1, 1])
        minus_half = sb("minus_half", [P, 1])
        ssq = sb("ssq", [P, TT])
        mean_sq = sb("mean_sq", [P, TT])
        rstd = sb("rstd", [P, TT])
        ssq2 = sb("ssq2", [P, TT])
        mean_sq2 = sb("mean_sq2", [P, TT])
        rstd2 = sb("rstd2", [P, TT])
        ssq3 = sb("ssq3", [P, TT])
        mean_sq3 = sb("mean_sq3", [P, TT])
        rstd3 = sb("rstd3", [P, TT])
        soft = sb("soft", [P, 4, 4])
        wr = sb("wr", [P, KD, NE])
        br = sb("br", [P, NE])
        iota_f = sb("iota_f", [P, NE])
        iota_b = sb("iota_b", [P, SLOTS], BF16)
        logit = sb("logit", [P, NE])
        top = sb("top", [P, 2, 8])
        top_i = sb("top_i", [P, 8], U32)
        top_f = sb("top_f", [P, 8])
        top_e = sb("top_e", [P, 2, 8])
        gate4 = sb("gate4", [P, TOPK])
        hit = sb("hit", [P, NE])
        picked = sb("picked", [P, 2, NE])
        picked_b = sb("picked_b", [P, 2, NE], BF16)
        so_far = sb("so_far", [P, NE])
        so_far_b = sb("so_far_b", [P, 2, NE], BF16)
        gatesT = sb("gatesT", [NE, P])
        place_e = sb("place_e", [P, TT])
        g_e = sb("g_e", [P, TT, 8], BF16)
        bias_e = sb("bias_e", [P, 2 * FT])
        pool_i = sb("pool_i", [P, 2], I32)
        slot_id = sb("slot_id", [P, 2])
        list_sb = sb("list_sb", [P, 2, 8])
        look = sb("look", [P, 2, 2])
        here = sb("here", [P, 2, 2])
        gone_g = sb("gone_g", [P, 2])
        gather_i = sb("gather_i", [P, 2], I32)
        scatter_i = sb("scatter_i", [P, 2], I32)
        cnt = sb("cnt", [P, NE])
        more_e = sb("more_e", [P, NE])
        incl = sb("incl", [P, NE])
        v_tab = sb("v_tab", [P, 4, VISITS + 1])
        v_int = sb("v_int", [P, 3, VISITS + 1], I32)
        n_vis = sb("n_vis", [P, 1], I32)

        bank = [ctx.enter_context(nc.psum_tensor(f"bank{i}", [P, HALF], F32)) for i in range(4)]
        wide = [ctx.enter_context(nc.psum_tensor(f"wide{i}", [P, 2 * HALF], F32)) for i in range(2)]

        def half(i):
            return bank[i][:, :] if i < 4 else wide[(i - 4) // 2][:, (i % 2) * HALF:(i % 2 + 1) * HALF]

        list_ps = half(7)[:, 0:16].rearrange("p (b n) -> p b n", b=2)

        names = """small_loaded consts_made idents_made iotas_made chain_pool chain_dve
            rows_turned cols_made c_sigmoid c_ready c_spread mod_summed mod_copied mod_turned scale1_made scale2_made gates_summed gate_made
            angles_made sines_made ssq_made rstd_made x_scaled x_turned h_even h_odd
            ag_summed a_copied sig_made u_made qkv_summed qkv_copied rot_summed rot_read q_rotated
            conv_made mean_summed centred squared var_summed var_made std_made z_made z_sigmoid conv_out
            scored score_masked exped prob_turned probT_act probT_dve weighed o_made attn_turned attn_made
            gate2_loaded b_down_loaded mixed mix_read x1_made ssq2_made rstd2_made xn_made xn_turned h2_low h2_high
            logits_summed top_made exp4_made picked_made gatesT_made bd_summed bd_read acc_made
            placed counted settles blanks_made tables_ready zeros_made
            list_made list_summed gather_ready gathered_a gathered_b x2_turned x2_made
            pair_summed g_made pair_read t_made s_made act_made y_summed y_copied y_turned y_made
            scattered_a scattered_b g_final_loaded sums_ready fin_ssq fin_rstd fin_made fin_stored xn_stored""".split()
        S = {n: sem(n) for n in names}
        dense_loaded = [sem(f"dense_loaded{i}") for i in range(RING1)]
        x_loaded = [sem(f"x_loaded{t}") for t in range(TT)]
        x_back = [sem(f"x_back{b}") for b in range(2)]
        acc_stored = [sem(f"acc_stored{b}") for b in range(2)]
        fin_loaded = [sem(f"fin_loaded{t}") for t in range(TT)]
        piece_loaded = [sem(f"piece_loaded{i}") for i in range(RING)]

        def columns(w, first):
            return w[:, first:first + PIECE].rearrange("(k p) n -> p k n", p=P)

        def rows(v, n=P):
            return v.rearrange("(q p) -> q p", p=n)

        dense = [(columns(w_ada, i * PIECE), "mod_summed", i + 1) for i in range(8)]
        AG = len(dense)
        dense += [(columns(w_in, first), "ag_summed", used)
                  for first, used in ((0, 7), (CH, 8), (PIECE, 15), (CH + PIECE, 16))]
        QK = len(dense)
        dense += [(columns(w_in, 2 * CH + i * PIECE), "qkv_summed", min(4 * (i + 1), 24) if i < 4 else 24) for i in range(6)]
        ADA2 = len(dense)
        dense += [(columns(w_ada, (8 + i) * PIECE), "gates_summed", i + 1) for i in range(4)]
        dense += [(columns(w_ada, (12 + i) * PIECE), "mod_summed", 9 + i) for i in range(8)]
        dense += [(columns(w_ada, (20 + i) * PIECE), "gates_summed", 5 + i) for i in range(4)]
        OUT = len(dense)
        dense += [(columns(w_out, i * PIECE), "mixed", TT) for i in range(4)]

        def dense_piece(n):
            return ring[:, n % RING1]

        def ring_slot(i):
            return (i + 6) % RING

        squares_after = {4: (0, 1), 5: (2, 3, 4, 5), 6: (6, 7)}
        variances_after = {5: (0, 1, 2, 3), 6: (4, 5, 6, 7)}

        block = ctx.enter_context(nc.Block())

        @block.sync
        def _(sp):
            sp.wait_ge(S["small_loaded"], 16 * 13)
            for n, (src, _, _) in enumerate(dense):
                if n < TT:
                    sp.dma_start(x_in[:, n, :], x[n * P:(n + 1) * P, :]).then_inc(x_loaded[n], 16)
                if n >= RING1:
                    sp.wait_ge(S[dense[n - RING1][1]], dense[n - RING1][2])
                sp.dma_start(dense_piece(n), src).then_inc(dense_loaded[n % RING1], 16)

            def expert_piece(e, i):
                w, first = (w_gu, (i // 2) * PIECE + (i % 2) * D) if i < 8 else (w_down, (i - 8) * PIECE)
                return w[bass.ds(e, 1), :, first:first + PIECE].rearrange("a (k p) n -> p (a k) n", p=P)

            def first_expert(i):
                slot = ring_slot(i)
                if slot < RING1:
                    last = max(n for n in range(len(dense)) if n % RING1 == slot)
                    sp.wait_ge(S[dense[last][1]], dense[last][2])
                else:
                    sp.wait_ge(S["scored"], TT * HEADS)
                sp.dma_start(ring[:, slot], expert_piece(0, i)).then_inc(piece_loaded[i], 16)

            def reload(t):
                if t >= 2:
                    sp.wait_ge(S["x1_made"], t - 1)
                sp.dma_start(x_again[:, t % 2, :], x[t * P:(t + 1) * P, :]).then_inc(x_back[t % 2], 16)

            def store_sums(t):
                sp.wait_ge(S["acc_made"], t + 1)
                sp.dma_start(sum_rows[t * P:(t + 1) * P, :], acc_sb[t % 2]).then_inc(acc_stored[t % 2], 16)

            sp.wait_ge(S["conv_out"], CT)
            reload(0)
            reload(1)
            w_out_slots = {n % RING1 for n in range(OUT, len(dense))}
            early = [i for i in range(RING) if ring_slot(i) not in w_out_slots]
            for i in early:
                first_expert(i)
            for t in range(TT + 2):
                if 1 <= t <= TT:
                    sp.wait_ge(S["xn_made"], t)
                    sp.dma_start(xn_rows[(t - 1) * P:t * P, :], xn1).then_inc(S["xn_stored"], 16)
                if t + 2 < TT:
                    reload(t + 2)
                if t >= 2:
                    store_sums(t - 2)
            for i in range(RING):
                if i not in early:
                    first_expert(i)
            sp.wait_ge(S["tables_ready"], 1)
            with sp.Fori(0, VISITS // GROUP) as group:
                at = sp.value_load(v_int[0:1, 1, bass.ds(group * GROUP, 1)], min_val=0, max_val=CLASSES)
                with sp.If(at > 0):
                    with sp.Fori(0, GROUP) as turn:
                        v = group * GROUP + turn
                        cls = sp.value_load(v_int[0:1, 1, bass.ds(v + 1, 1)], min_val=0, max_val=CLASSES)
                        with sp.If(cls > 0):
                            e = sp.value_load(v_int[0:1, 0, bass.ds(v + 1, 1)], min_val=0, max_val=NE - 1)
                            for i in range(RING):
                                if i < 8:
                                    sp.wait_ge(S["pair_summed"], v * FT + 2 * (i // 2 + 1))
                                else:
                                    sp.wait_ge(S["y_summed"], v * KD + 2 * (i - 7))
                                sp.dma_start(ring[:, ring_slot(i)], expert_piece(e, i)).then_inc(piece_loaded[i], 16)
            sp.wait_ge(S["sums_ready"], 1)
            for t in range(TT):
                sp.dma_start(fin[:, t, :], sum_rows[t * P:(t + 1) * P, :]).then_inc(fin_loaded[t], 16)
            for t in range(TT):
                sp.wait_ge(S["fin_made"], t + 1)
                sp.dma_start(out[t * P:(t + 1) * P, :], fin[:, t, :]).then_inc(S["fin_stored"], 16)
            sp.wait_ge(S["fin_stored"], 16 * TT)

        @block.gpsimd
        def _(pool):
            link = Chain(pool, S["chain_pool"])
            G = nc.gpsimd

            def diagonal(m, view, value, base, pattern):
                link(G.affine_select(out=view, in_=view, compare_op=ALU.not_equal, fill=value, base=base, pattern=pattern,
                                     channel_multiplier=1))

            link(G.memset(ident[:, :], 0.0))
            diagonal(ident, ident[:, :], 1.0, 0, [[-1, P]])
            G.memset(freq_row[0:1, :], 0.0)
            G.memset(minus_half[:, :], -0.5)
            link(G.memset(ones[:, :], 1.0))
            inv_freq = np.float32(THETA) ** (-(np.arange(0, ROT, 2, dtype=np.float32) / np.float32(ROT)))
            fr = freq_row[0:1, :].rearrange("a (h n) -> a h n", h=2)
            for j in range(ROT):
                ins = G.memset(fr[:, :, j:j + 1], float(inv_freq[j % (ROT // 2)]))
            ins.then_inc(S["idents_made"], 1)
            G.iota(tmp[3].bitcast(I32), pattern=[[-1, T]], base=T - P, channel_multiplier=1).then_inc(S["iotas_made"], 1)
            G.iota(iota_i, pattern=[[1, SLOTS]], base=0, channel_multiplier=0).then_inc(S["iotas_made"], 1)
            link(G.memset(rot_m[:, :], 0.0))
            rv = rot_m[:, :].rearrange("p (h n) -> p h n", h=2)
            diagonal(rot_m, rv[:, :, 0:8], -1.0, -8, [[-HD, 2], [-1, 8]])
            diagonal(rot_m, rv[:, :, 8:16], 1.0, 0, [[-HD, 2], [-1, 8]])
            link(G.memset(before_m[:, :], 1.0))
            link(G.affine_select(out=before_m[:, :], in_=before_m[:, :], compare_op=ALU.is_gt, fill=0.0, base=0,
                                 pattern=[[1, P]], channel_multiplier=-1))
            G.memset(ones_b[:, :], 1.0)
            link(G.iota(pool_i[:, :], pattern=[[P, 2]], base=T, channel_multiplier=1))
            link(G.tensor_copy(slot_id[:, :], pool_i[:, :]))
            G.memset(v_tab[:, 3, 0:NE], 0.0)
            G.memset(v_tab[:, 3, VISITS:VISITS + 1], NEVER)
            G.memset(v_tab[:, 0:2, VISITS:VISITS + 1], 0.0)
            G.memset(here[:, :, :], 0.0).then_inc(S["consts_made"], 1)

            def rsqrt_mean(t, sums, mean, result, ready, done):
                pool.wait_ge(S[ready], t + 1)
                link(G.tensor_scalar(mean[:, t:t + 1], sums[:, t:t + 1], 1.0 / D, EPS, ALU.mult, ALU.add))
                G.tensor_tensor(result[:, t:t + 1], mean[:, t:t + 1], minus_half[:, :], ALU.pow).then_inc(S[done], 1)

            for t in range(TT):
                rsqrt_mean(t, ssq, mean_sq, rstd, "ssq_made", "rstd_made")

            pool.wait_ge(S["conv_out"], CT)
            pool.dma_start(gate2_b, b_ada[5 * D:6 * D].partition_broadcast(P)).then_inc(S["gate2_loaded"], 16)
            pool.wait_ge(S["q_rotated"], 4 * QT)
            pool.dma_start(b_down_sb, b_down).then_inc(S["b_down_loaded"], 16)
            rest_i = g_rest.rearrange("p t e -> p (t e)").bitcast(I32)
            pool.wait_ge(S["score_masked"], TT * HEADS)
            for col, pattern, step in ((0, [[0, TT * NE]], 1), (1, [[P, TT], [0, NE]], 0)):
                link(G.iota(rest_i, pattern=pattern, base=0, channel_multiplier=step))
                link(G.tensor_copy(g_cols[:, :, :, col], g_rest.bitcast(I32)))
            G.memset(g_cols[:, :, :, 2:3], 1.0)
            G.memset(g_cols[:, :, :, 6:8], 0.0).then_inc(S["consts_made"], 1)
            pool.wait_ge(S["zeros_made"], 2)
            for b, done in enumerate(("scattered_a", "scattered_b")):
                pool.dma_start(sum_rows[T + b * P:T + (b + 1) * P, :], x1[2]).then_inc(S[done], 16)
            for t in range(TT):
                rsqrt_mean(t, ssq2, mean_sq2, rstd2, "ssq2_made", "rstd2_made")
            pool.wait_ge(S["mixed"], TT)
            G.memset(yT[:, :, :], 0.0).then_inc(S["blanks_made"], 1)
            for b in range(2):
                pool.wait_ge(acc_stored[b], 16 * TT // 2)
            for buf in got:
                G.memset(buf, 0.0).then_inc(S["blanks_made"], 1)
            pool.wait_ge(S["xn_stored"], 16 * TT)
            pool.wait_ge(S["scattered_a"], 16)
            pool.wait_ge(S["scattered_b"], 16)

            def settle(before=None):
                if before is not None:
                    pool.wait_ge(S["settles"], before)
                G.tensor_tensor(settled[:, :], minus_half[0:1, :], minus_half[0:1, :], ALU.add).then_inc(S["settles"], 1)

            def gather(n, before=None):
                pool.wait_ge(S["gather_ready"], n + 1)
                settle(before)
                for b, done in enumerate(("gathered_a", "gathered_b")):
                    pool.indirect_dma_start(got[b], None, xn_rows, bass.IndirectOffsetOnAxis(ap=gather_i[:, b:b + 1], axis=0),
                                            bounds_check=T - 1, oob_is_err=False).then_inc(S[done], 16)

            def scatter(n):
                for b, done in enumerate(("scattered_a", "scattered_b")):
                    pool.wait_ge(S["y_made"], n * 4 + (2 * b + 2))
                    settle(n * 3 + (b + 1))
                    pool.indirect_dma_start(sum_rows, bass.IndirectOffsetOnAxis(ap=scatter_i[:, b:b + 1], axis=0), y_nat[b], None,
                                            bounds_check=T + SLOTS - 1, oob_is_err=True, compute_op=ALU.add).then_inc(S[done], 16)

            pool.dma_start(g_fin_b, g_final.partition_broadcast(P)).then_inc(S["g_final_loaded"], 16)
            gather(0)
            with pool.Fori(0, VISITS // GROUP) as group:
                at = pool.value_load(v_int[0:1, 1, bass.ds(group * GROUP, 1)], min_val=0, max_val=CLASSES)
                with pool.If(at > 0):
                    with pool.Fori(0, GROUP) as turn:
                        v = group * GROUP + turn
                        cls = pool.value_load(v_int[0:1, 1, bass.ds(v, 1)], min_val=0, max_val=CLASSES)
                        with pool.If(cls > 0):
                            scatter(v)
                            gather(v + 1, v * 3 + 3)
            n = pool.value_load(n_vis[0:1, 0:1], min_val=NE, max_val=VISITS)
            scatter(n)
            pool.wait_ge(S["scattered_a"], n * 16 + 32)
            settle(n * 3 + 3)
            pool.wait_ge(S["scattered_b"], n * 16 + 32)
            settle(n * 3 + 4)
            G.memset(mean_sq3[:, :], 0.0).then_inc(S["sums_ready"], 1)
            pool.wait_ge(S["sums_ready"], 1)
            for t in range(TT):
                rsqrt_mean(t, ssq3, mean_sq3, rstd3, "fin_ssq", "fin_rstd")

        @block.scalar
        def _(act):
            A = nc.scalar
            first = 0
            for src, n in ((c, 8), (b_ada, 48), (g_mix, 8), (g_ffn, 8), (conv_b, 4), (conv_ln_g, 4), (conv_ln_b, 4)):
                act.dma_start(row_a[first:first + n, :], rows(src)).then_inc(S["small_loaded"], 16)
                first += n
            act.dma_start(row_c[0:TAPS * CT, :], rows(conv_w)).then_inc(S["small_loaded"], 16)
            act.dma_start(row_g[:, :, :], b_gu.rearrange("(q r p) -> r q p", r=P, p=P)).then_inc(S["small_loaded"], 16)
            act.dma_start(tmp[0].bitcast(I32), positions.partition_broadcast(P)).then_inc(S["small_loaded"], 16)
            act.dma_start(wr[:, :, :], w_router.rearrange("(k p) n -> p k n", p=P)).then_inc(S["small_loaded"], 16)
            act.dma_start(br[:, :], b_router.partition_broadcast(P)).then_inc(S["small_loaded"], 16)
            act.dma_start(gate1_b[:, :], b_ada[2 * D:3 * D].partition_broadcast(P)).then_inc(S["small_loaded"], 16)

            act.wait_ge(S["cols_made"], 1)
            A.activation(c_sigm[:, :], cols[:, 0:KD], ACT.Sigmoid).then_inc(S["c_sigmoid"], 1)
            act.wait_ge(S["angles_made"], 1)
            A.activation(sin_t, tmp[1], ACT.Sin)
            A.activation(cos_t, tmp[2], ACT.Sin).then_inc(S["sines_made"], 1)
            for t in range(TT):
                act.wait_ge(x_loaded[t], 16)
                if t >= 1:
                    act.wait_ge(S["ssq_made"], t)
                A.activation(hT[:, 0, :], x_in[:, t, :], ACT.Square, accum_out=ssq[:, t:t + 1]).then_inc(S["ssq_made"], 1)
            act.wait_ge(S["scale1_made"], 1)
            act.wait_ge(S["ssq_made"], TT)
            for n in range(0, 2 * KD, 2):
                g, k = n // KD, n % KD
                act.wait_ge(S["x_turned"], n + 1)
                A.activation(hT[:, k, g * HALF:(g + 1) * HALF], half(n % 4), ACT.Identity, scale=scale1[:, k:k + 1],
                             bias=mod1[:, k:k + 1]).then_inc(S["h_even"], 1)
            for i in range(2 * CT):
                ct, h = i // 2, i % 2
                act.wait_ge(S["ag_summed"], 2 * i + 1)
                A.copy(u_pad[:, ct, TAPS - 1 + h * HALF:TAPS - 1 + (h + 1) * HALF], half(4 + (2 * i) % 4)).then_inc(S["a_copied"], 1)
                act.wait_ge(S["ag_summed"], 2 * i + 2)
                A.activation(sig_g[:, ct, h * HALF:(h + 1) * HALF], half(4 + (2 * i + 1) % 4), ACT.Sigmoid).then_inc(S["sig_made"], 1)
            for i in range(4 * QT):
                dst, f = (qT, i // 2) if i < 2 * QT else (kT, i // 2 - QT)
                act.wait_ge(S["qkv_summed"], i + 1)
                A.copy(dst[:, f, (i % 2) * HALF:(i % 2 + 1) * HALF], half(i % 2)).then_inc(S["qkv_copied"], 1)
            act.wait_ge(S["u_made"], 2 * CT)
            for t in range(TT):
                act.wait_ge(S["qkv_summed"], 4 * QT + t + 1)
                A.copy(v_nat[:, t, :], half(t % 2)).then_inc(S["qkv_copied"], 1)
                for i in squares_after.get(t, ()):
                    h, ct = i // CT, i % CT
                    act.wait_ge(S["centred"], i + 1)
                    if i >= 2:
                        act.wait_ge(S["var_summed"], i - 1)
                    A.activation(norm_tmp[2 + i % 2][:, 0:HALF], conv[:, ct, h * HALF:(h + 1) * HALF], ACT.Square).then_inc(S["squared"], 1)
            act.wait_ge(S["var_made"], 1)
            A.activation(norm_tmp[0], norm_tmp[1], ACT.Sqrt).then_inc(S["std_made"], 1)
            for ct in range(CT):
                act.wait_ge(S["z_made"], ct + 1)
                if ct >= 2:
                    act.wait_ge(S["conv_out"], ct - 1)
                A.activation(norm_tmp[2 + ct % 2], conv[:, ct, :], ACT.Sigmoid).then_inc(S["z_sigmoid"], 1)

            def copy_turned(i):
                act.wait_ge(S["prob_turned"], i + 1)
                if i >= 2:
                    act.wait_ge(S["weighed"], i - 1)
                m = min((i // HEADS + 1) * P, HALF)
                A.copy(probT[i % 2][:, 0:m], half(0)[:, 0:m]).then_inc(S["probT_act"], 1)

            def copy_attn(qt):
                act.wait_ge(S["attn_turned"], qt + 1)
                A.copy(attnT[:, :, qt * P:(qt + 1) * P], half(3).rearrange("p (f t) -> p f t", f=QT)).then_inc(S["attn_made"], 1)

            ITEMS = TT * HEADS
            for i in range(ITEMS):
                n = (i // HEADS + 1) * P
                act.wait_ge(S["score_masked"], i + 1)
                A.activation(prob[i % 2][:, 0:n], prob[i % 2][:, 0:n], ACT.Exp, scale=HD ** -0.5, bias=soft[:, i % 4, 1:2],
                             accum_out=soft[:, i % 4, 2:3]).then_inc(S["exped"], 1)
                if i >= 1:
                    copy_turned(i - 1)
                if i > HEADS and i % HEADS == 4:
                    copy_attn(i // HEADS - 1)
            copy_turned(ITEMS - 1)
            copy_attn(TT - 1)

            for t in range(TT + 1):
                if t >= 1:
                    b = (t - 1) % 2
                    act.wait_ge(S["xn_turned"], t)
                    for k in range(KD // 2):
                        ins = A.activation(h2T[b][:, k, :], wide[1][:, k * P:(k + 1) * P], ACT.Identity, scale=scale2[:, k:k + 1],
                                           bias=mod2[:, k:k + 1])
                    ins.then_inc(S["h2_low"], 1)
                if t < TT:
                    act.wait_ge(S["x1_made"], t + 1)
                    if t >= 1:
                        act.wait_ge(S["ssq2_made"], t)
                    A.activation(square, x1[t % 3], ACT.Square, accum_out=ssq2[:, t:t + 1]).then_inc(S["ssq2_made"], 1)
                if t >= 1:
                    act.wait_ge(S["top_made"], t)
                    A.activation(top_e[:, b, 0:TOPK], top[:, b, 0:TOPK], ACT.Exp, bias=top_e[:, b, 4:5],
                                 accum_out=top_e[:, b, 5:6]).then_inc(S["exp4_made"], 1)

            def turn_x(n, tiles):
                for k in tiles:
                    if k % 2 == 0:
                        act.wait_ge(S["x2_turned"], n * 4 + (k // 2 + 1))
                    ins = A.activation(xT[:, k, :], wide[0][:, (k % 4) * SLOTS:(k % 4 + 1) * SLOTS], ACT.Identity,
                                       scale=scale2[:, k:k + 1], bias=mod2[:, k:k + 1])
                    if k % 2:
                        ins.then_inc(S["x2_made"], 1)

            act.wait_ge(S["tables_ready"], 1)
            for m in range(2):
                A.copy(yT[:, m, 0:1], yT[:, m, 1:2]).then_inc(S["y_copied"], 1)
            turn_x(0, range(KD))
            with act.Fori(0, VISITS // GROUP) as group:
                at = act.value_load(v_int[0:1, 1, bass.ds(group * GROUP, 1)], min_val=0, max_val=CLASSES)
                with act.If(at > 0):
                    with act.Fori(0, GROUP) as turn:
                        v = group * GROUP + turn
                        cls = act.value_load(v_int[0:1, 1, bass.ds(v, 1)], min_val=0, max_val=CLASSES)
                        with act.If(cls > 0):
                            for j in range(FT):
                                act.wait_ge(S["g_made"], v * FT + (j + 1))
                                A.activation(s_buf[:, j % 2, :], g_buf[:, j % 2, :], ACT.Sigmoid, scale=ALPHA).then_inc(S["s_made"], 1)
                            turn_x(v + 1, range(KD // 2))
                            for m in range(KD):
                                act.wait_ge(S["y_summed"], v * KD + (m + 1))
                                A.copy(yT[:, m, :], half(6 + m % 2)[:, 0:SLOTS]).then_inc(S["y_copied"], 1)
                                if m == 0:
                                    turn_x(v + 1, range(KD // 2, KD))
            for t in range(TT):
                act.wait_ge(fin_loaded[t], 16)
                if t >= 2:
                    act.wait_ge(S["fin_ssq"], t - 1)
                A.activation(fin_square[:, t % 2, :], fin[:, t, :], ACT.Square, accum_out=ssq3[:, t:t + 1]).then_inc(S["fin_ssq"], 1)

        @block.vector
        def _(dve):
            link = Chain(dve, S["chain_dve"])
            V = nc.vector
            dve.wait_ge(S["iotas_made"], 2)
            V.tensor_copy(iota_b[:, :], iota_i)
            V.tensor_copy(iota_f[:, :], iota_i[:, 0:NE])
            dve.wait_ge(S["rows_turned"], 1)
            V.tensor_copy(cols[:, :], bank[0][:, 0:84])
            V.tensor_copy(conv_cols[:, :], bank[0][:, P:P + TAPS * CT])
            V.tensor_copy(freq[:, :], bank[0][:, 2 * P:2 * P + 1])
            link(V.tensor_copy(bgu[:, :, :].rearrange("p e j -> p (e j)"), bank[1][:, :]))
            V.tensor_scalar(bgu[:, :, FT:2 * FT], bgu[:, :, FT:2 * FT], 1.0, None, ALU.add).then_inc(S["cols_made"], 1)
            dve.wait_ge(S["c_sigmoid"], 1)
            V.tensor_tensor(c_act[:, :], cols[:, 0:KD], c_sigm[:, :], ALU.mult).then_inc(S["c_ready"], 1)
            dve.wait_ge(S["c_ready"], 1)
            for k in range(KD):
                ins = V.tensor_scalar(c_bc[:, k, :], ones[:, :], c_act[:, k:k + 1], None, ALU.mult)
            ins.then_inc(S["c_spread"], 1)
            dve.wait_ge(S["small_loaded"], 16 * 13)
            link(V.tensor_copy(tmp[1], tmp[0].bitcast(I32)))
            link(V.tensor_scalar(tmp[0], tmp[1], freq[:, 0:1], None, ALU.mult))
            link(V.tensor_scalar(tmp[1], tmp[0], 1.0 / (2 * math.pi), None, ALU.mult))
            link(V.tensor_scalar(tmp[1], tmp[1], ROUND, None, ALU.add))
            link(V.tensor_scalar(tmp[1], tmp[1], -ROUND, None, ALU.add))
            for two_pi in (TWO_PI_A, TWO_PI_B, TWO_PI_C):
                link(V.scalar_tensor_tensor(out=tmp[0], in0=tmp[1], scalar=-two_pi, in1=tmp[0], op0=ALU.mult, op1=ALU.add))
            link(V.tensor_scalar(tmp[1], tmp[0], 3.1415925, -3.1415925, ALU.min, ALU.max))
            link(V.tensor_scalar(tmp[2], tmp[1], -1.0, None, ALU.mult))
            link(V.tensor_tensor(tmp[2], tmp[1], tmp[2], ALU.min))
            V.tensor_scalar(tmp[2], tmp[2], math.pi / 2, None, ALU.add).then_inc(S["angles_made"], 1)
            dist = tmp[3].bitcast(I32)
            dve.wait_ge(S["sines_made"], 1)
            link(V.tensor_scalar(tmp[1], dist, 0.0, None, ALU.is_ge))
            link(V.scalar_tensor_tensor(out=mask, in0=dist, scalar=float(P), in1=tmp[1], op0=ALU.is_le, op1=ALU.mult))
            for low, window in ((3, 512), (15, 2048)):
                link(V.tensor_scalar(tmp[0].bitcast(I32), dist, low, None, ALU.bitwise_and))
                link(V.scalar_tensor_tensor(out=tmp[0], in0=tmp[0].bitcast(I32), scalar=0.0, in1=tmp[1], op0=ALU.is_equal, op1=ALU.mult))
                link(V.scalar_tensor_tensor(out=tmp[0], in0=dist, scalar=float(window), in1=tmp[0], op0=ALU.is_le, op1=ALU.mult))
                link(V.tensor_tensor(mask, mask, tmp[0], ALU.add))
            link(V.tensor_scalar(tmp[0], mask, 2.0, 8 * math.log(2.0), ALU.is_ge, ALU.mult))
            link(V.tensor_scalar(tmp[1], mask, 3.0, 8 * math.log(1.5), ALU.is_ge, ALU.mult))
            link(V.tensor_tensor(tmp[0], tmp[0], tmp[1], ALU.add))
            link(V.tensor_scalar(tmp[1], mask, 1.0, -BIG, ALU.is_lt, ALU.mult))
            link(V.tensor_tensor(mask, tmp[0], tmp[1], ALU.add))
            for ct in range(CT):
                ins = V.memset(u_pad[:, ct, 0:TAPS - 1], 0.0)
            link(ins)
            V.memset(top_e[:, 0, 6:8], 0.0).then_inc(S["zeros_made"], 1)
            for t in range(TT):
                dve.wait_ge(S["rstd_made"], t + 1)
                V.tensor_scalar(x_in[:, t, :], x_in[:, t, :], rstd[:, t:t + 1], None, ALU.mult).then_inc(S["x_scaled"], 1)
            def copy_mod(done):
                for i in range(4):
                    dve.wait_ge(S["mod_summed"], done + 2 * (i + 1))
                    V.tensor_copy(mod_row[:, i * HALF:(i + 1) * HALF], bank[i][0:1, :]).then_inc(S["mod_copied"], 1)

            copy_mod(0)
            dve.wait_ge(S["mod_turned"], 1)
            link(V.tensor_tensor(mod1[:, :], bank[2][:, 0:2 * KD], cols[:, C_ADA:C_ADA + 2 * KD], ALU.add))
            link(V.tensor_scalar(scale1[:, :], mod1[:, KD:2 * KD], 1.0, None, ALU.add))
            V.tensor_tensor(scale1[:, :], scale1[:, :], cols[:, C_MIX:C_MIX + KD], ALU.mult).then_inc(S["scale1_made"], 1)
            dve.wait_ge(S["scale1_made"], 1)
            dve.wait_ge(S["ssq_made"], TT)
            for n in range(1, 2 * KD, 2):
                g, k = n // KD, n % KD
                dve.wait_ge(S["x_turned"], n + 1)
                V.tensor_scalar(hT[:, k, g * HALF:(g + 1) * HALF], half(n % 4), scale1[:, k:k + 1], mod1[:, k:k + 1],
                                ALU.mult, ALU.add).then_inc(S["h_odd"], 1)
            for ct in range(CT):
                for h in range(2):
                    dve.wait_ge(S["a_copied"], 2 * ct + h + 1)
                    dve.wait_ge(S["sig_made"], 2 * ct + h + 1)
                    uv = u_pad[:, ct, TAPS - 1 + h * HALF:TAPS - 1 + (h + 1) * HALF]
                    V.tensor_tensor(uv, uv, sig_g[:, ct, h * HALF:(h + 1) * HALF], ALU.mult).then_inc(S["u_made"], 1)
                dve.wait_ge(S["u_made"], 2 * ct + 2)
                for w in range(TAPS):
                    src, tap = u_pad[:, ct, w:w + T], conv_cols[:, w * CT + ct:w * CT + ct + 1]
                    if w == 0:
                        link(V.tensor_scalar(conv[:, ct, :], src, tap, cols[:, C_CB + ct:C_CB + ct + 1], ALU.mult, ALU.add))
                        continue
                    ins = V.scalar_tensor_tensor(out=conv[:, ct, :], in0=src, scalar=tap, in1=conv[:, ct, :], op0=ALU.mult, op1=ALU.add)
                    if w < TAPS - 1:
                        link(ins)
                ins.then_inc(S["conv_made"], 1)
            def centre():
                for i in range(2 * CT):
                    h, ct = i // CT, i % CT
                    dve.wait_ge(S["mean_summed"], h + 1)
                    yv = conv[:, ct, h * HALF:(h + 1) * HALF]
                    V.scalar_tensor_tensor(out=yv, in0=half(4 + h), scalar=-1.0 / CH, in1=yv, op0=ALU.mult,
                                           op1=ALU.add).then_inc(S["centred"], 1)

            dve.wait_ge(S["conv_made"], CT)
            for i in range(4 * QT):
                dst, f = (qT, i // 2) if i < 2 * QT else (kT, i // 2 - QT)
                hs = slice((i % 2) * HALF, (i % 2 + 1) * HALF)
                dve.wait_ge(S["rot_summed"], i + 1)
                V.tensor_tensor(rot_tmp[i % 2], half(2 + i % 2), sin_t[:, hs], ALU.mult).then_inc(S["rot_read"], 1)
                link(V.tensor_tensor(dst[:, f, hs], dst[:, f, hs], cos_t[:, hs], ALU.mult))
                dve.wait_ge(S["rot_read"], i + 1)
                V.tensor_tensor(dst[:, f, hs], dst[:, f, hs], rot_tmp[i % 2], ALU.add).then_inc(S["q_rotated"], 1)
                if i == 9:
                    centre()
            dve.wait_ge(S["var_summed"], 2 * CT)
            dve.wait_ge(S["q_rotated"], 4 * QT)
            V.tensor_scalar(norm_tmp[1], wide[1][:, :], 1.0 / CH, EPS, ALU.mult, ALU.add).then_inc(S["var_made"], 1)
            dve.wait_ge(S["gates_summed"], 4)
            V.tensor_tensor(gate1_b[:, :], gate1_b[:, :], wide[0][:, :], ALU.add).then_inc(S["gate_made"], 1)
            dve.wait_ge(S["centred"], 2 * CT)
            dve.wait_ge(S["std_made"], 1)
            link(V.reciprocal(norm_tmp[1], norm_tmp[0]))
            for ct in range(CT):
                link(V.tensor_tensor(conv[:, ct, :], conv[:, ct, :], norm_tmp[1], ALU.mult))
                V.tensor_scalar(conv[:, ct, :], conv[:, ct, :], cols[:, C_LG + ct:C_LG + ct + 1], cols[:, C_LB + ct:C_LB + ct + 1],
                                ALU.mult, ALU.add).then_inc(S["z_made"], 1)
            for ct in range(CT):
                dve.wait_ge(S["z_sigmoid"], ct + 1)
                V.tensor_tensor(conv[:, ct, :], conv[:, ct, :], norm_tmp[2 + ct % 2], ALU.mult).then_inc(S["conv_out"], 1)
            copy_mod(8)
            dve.wait_ge(S["mod_turned"], 2)
            link(V.tensor_tensor(mod2[:, :], bank[2][:, 0:2 * KD], cols[:, C_ADA + 3 * KD:C_ADA + 5 * KD], ALU.add))
            link(V.tensor_scalar(scale2[:, :], mod2[:, KD:2 * KD], 1.0, None, ALU.add))
            V.tensor_tensor(scale2[:, :], scale2[:, :], cols[:, C_FFN:C_FFN + KD], ALU.mult).then_inc(S["scale2_made"], 1)
            dve.wait_ge(S["gates_summed"], 8)
            dve.wait_ge(S["gate2_loaded"], 16)
            V.tensor_tensor(gate2_b, gate2_b, wide[0][:, :], ALU.add).then_inc(S["gate_made"], 1)

            def copy_turned(i):
                n = (i // HEADS + 1) * P
                if n > HALF:
                    dve.wait_ge(S["prob_turned"], i + 1)
                    dve.wait_ge(S["weighed"], i - 1)
                    V.tensor_copy(probT[i % 2][:, HALF:n], half(1)[:, 0:n - HALF]).then_inc(S["probT_dve"], 1)

            def normalise(i):
                qt, h = i // HEADS, i % HEADS
                dve.wait_ge(S["weighed"], i + 1)
                if qt >= 2 and h == 0:
                    dve.wait_ge(S["attn_turned"], qt - 1)
                link(V.reciprocal(soft[:, i % 4, 3:4], soft[:, i % 4, 2:3]))
                V.tensor_scalar(o_nat[qt % 2][:, h * HD:(h + 1) * HD], half(2 + i % 2)[:, h * HD:(h + 1) * HD], soft[:, i % 4, 3:4], None,
                                ALU.mult).then_inc(S["o_made"], 1)

            ITEMS = TT * HEADS
            for i in range(ITEMS):
                n = (i // HEADS + 1) * P
                dve.wait_ge(S["scored"], i + 1)
                if i >= 2:
                    dve.wait_ge(S["prob_turned"], i - 1)
                link(V.tensor_tensor_reduce(out=prob[i % 2][:, 0:n], in0=wide[i % 2][:, 0:n], in1=mask[:, T - n:T], scale=1.0,
                                            scalar=-3e38, op0=ALU.add, op1=ALU.max, accum_out=soft[:, i % 4, 0:1]))
                V.tensor_scalar(soft[:, i % 4, 1:2], soft[:, i % 4, 0:1], -(HD ** -0.5), None, ALU.mult).then_inc(S["score_masked"], 1)
                if i >= 1:
                    copy_turned(i - 1)
                if i >= 2:
                    normalise(i - 2)
            copy_turned(ITEMS - 1)
            normalise(ITEMS - 2)
            normalise(ITEMS - 1)

            def normalise_rows(t):
                dve.wait_ge(S["rstd2_made"], t + 1)
                if t >= 1:
                    dve.wait_ge(S["xn_turned"], t)
                    dve.wait_ge(S["xn_stored"], 16 * t)
                V.tensor_scalar(xn1, x1[t % 3], rstd2[:, t:t + 1], None, ALU.mult).then_inc(S["xn_made"], 1)

            def weigh_mix(t):
                dve.wait_ge(S["mixed"], t + 1)
                if t == 2:
                    dve.wait_ge(S["scattered_a"], 16)
                    dve.wait_ge(S["scattered_b"], 16)
                if t >= 3:
                    dve.wait_ge(S["acc_made"], t - 2)
                V.tensor_tensor(x1[t % 3], wide[0][:, :], gate1_b[:, :], ALU.mult).then_inc(S["mix_read"], 1)

            def residual(t):
                dve.wait_ge(x_back[t % 2], 16 * (t // 2 + 1))
                dve.wait_ge(S["mix_read"], t + 1)
                V.tensor_tensor(x1[t % 3], x1[t % 3], x_again[:, t % 2, :], ALU.add).then_inc(S["x1_made"], 1)

            def modulate(t):
                b = t % 2
                dve.wait_ge(S["xn_turned"], t + 1)
                for k in range(KD // 2, KD):
                    ins = V.tensor_scalar(h2T[b][:, k, :], wide[1][:, k * P:(k + 1) * P], scale2[:, k:k + 1], mod2[:, k:k + 1],
                                          ALU.mult, ALU.add)
                ins.then_inc(S["h2_high"], 1)

            def route(t):
                b = t % 2
                dve.wait_ge(S["logits_summed"], t + 1)
                link(V.tensor_tensor(logit[:, :], bank[0][:, 0:NE], br[:, :], ALU.add))
                link(V.max(out=top[:, b, :], in_=logit[:, :]))
                V.tensor_scalar(top_e[:, b, 4:5], top[:, b, 0:1], -1.0, None, ALU.mult).then_inc(S["top_made"], 1)
                link(V.max_index(out=top_i[:, :], in_max=top[:, b, :], in_values=logit[:, :]))
                link(V.tensor_copy(top_f[:, :], top_i[:, :]))
                dve.wait_ge(S["exp4_made"], t + 1)
                link(V.reciprocal(top_e[:, b, 6:7], top_e[:, b, 5:6]))
                link(V.tensor_scalar(gate4[:, :], top_e[:, b, 0:TOPK], top_e[:, b, 6:7], None, ALU.mult))
                for k in range(TOPK):
                    link(V.tensor_scalar(hit[:, :], iota_f[:, :], top_f[:, k:k + 1], None, ALU.is_equal))
                    if k == 0:
                        link(V.tensor_scalar(gates[:, t, :], hit[:, :], gate4[:, 0:1], None, ALU.mult))
                        link(V.tensor_copy(picked[:, b, :], hit[:, :]))
                    else:
                        link(V.scalar_tensor_tensor(out=gates[:, t, :], in0=hit[:, :], scalar=gate4[:, k:k + 1], in1=gates[:, t, :],
                                                    op0=ALU.mult, op1=ALU.add))
                        link(V.tensor_tensor(picked[:, b, :], picked[:, b, :], hit[:, :], ALU.add))
                V.tensor_copy(picked_b[:, b, :], picked[:, b, :])
                V.tensor_copy(so_far_b[:, b, :], so_far[:, :]).then_inc(S["picked_made"], 1)
                link(V.tensor_tensor(so_far[:, :], so_far[:, :], picked[:, b, :], ALU.add))

            def copy_gates(t):
                dve.wait_ge(S["placed"], t + 1)
                V.tensor_copy(gatesT[:, :], bank[3][0:NE, P:2 * P]).then_inc(S["gatesT_made"], 1)

            def enlist(t):
                b = t % 2
                link(V.scalar_tensor_tensor(out=place[:, t, :], in0=bank[3][:, 2 * P:2 * P + NE], scalar=-NEVER, in1=picked[:, b, :],
                                            op0=ALU.add, op1=ALU.mult))
                link(V.tensor_scalar(place[:, t, :], place[:, t, :], NEVER, None, ALU.add))
                dve.wait_ge(S["bd_summed"], 2 * t + 2)
                if t >= 2:
                    dve.wait_ge(acc_stored[b], 16 * (t // 2))
                for h in range(2):
                    hs = slice(h * HALF, (h + 1) * HALF)
                    V.tensor_tensor(acc_sb[b][:, hs], half(1 + h), gate2_b[:, hs], ALU.mult).then_inc(S["bd_read"], 1)
                dve.wait_ge(S["bd_read"], 2 * t + 2)
                V.tensor_tensor(acc_sb[b], acc_sb[b], x1[t % 3], ALU.add).then_inc(S["acc_made"], 1)

            dve.wait_ge(S["o_made"], ITEMS)
            dve.wait_ge(S["weighed"], ITEMS)
            V.memset(x1[2], 0.0).then_inc(S["zeros_made"], 1)
            link(V.memset(so_far[:, :], 0.0))
            for t in range(TT + 2):
                if 1 <= t <= TT:
                    normalise_rows(t - 1)
                if t >= 2:
                    copy_gates(t - 2)
                if t < TT:
                    weigh_mix(t)
                if 1 <= t <= TT:
                    modulate(t - 1)
                if t < TT:
                    residual(t)
                if t >= 2:
                    enlist(t - 2)
                if 1 <= t <= TT:
                    route(t - 1)

            V.tensor_copy(so_far_b[:, 0, :], so_far[:, :]).then_inc(S["picked_made"], 1)
            dve.wait_ge(S["consts_made"], 2)
            link(V.tensor_copy(g_cols[:, :, :, 3], gates))
            link(V.tensor_tensor(g_rest, gates, g_cols[:, :, :, 3], ALU.subtract))
            link(V.tensor_copy(g_cols[:, :, :, 4], g_rest))
            link(V.tensor_tensor(g_rest, g_rest, g_cols[:, :, :, 4], ALU.subtract))
            link(V.tensor_copy(g_cols[:, :, :, 5], g_rest))
            V.tensor_copy(here[:, 0, :], slot_id[:, :])
            link(V.memset(wide[1][:, :], 0.0))
            dve.wait_ge(S["counted"], 1)
            link(V.tensor_copy(cnt[:, :], bank[3][:, 3 * P:3 * P + NE]))
            link(V.tensor_scalar(v_tab[:, 1, 0:NE], cnt[:, :], float(WIDTHS[0]), 1.0, ALU.is_gt, ALU.add))
            for width in WIDTHS[1:-1]:
                link(V.scalar_tensor_tensor(out=v_tab[:, 1, 0:NE], in0=cnt[:, :], scalar=float(width), in1=v_tab[:, 1, 0:NE], op0=ALU.is_gt, op1=ALU.add))
            link(V.tensor_scalar(more_e[:, :], cnt[:, :], float(SLOTS), None, ALU.is_gt))
            for q in (2.0 * SLOTS, 3.0 * SLOTS):
                link(V.scalar_tensor_tensor(out=more_e[:, :], in0=cnt[:, :], scalar=q, in1=more_e[:, :], op0=ALU.is_gt, op1=ALU.add))
            link(V.memset(hit[:, :], 0.0))
            link(V.tensor_tensor_scan(out=incl[:, :], data0=more_e[:, :], data1=hit[:, :], initial=0.0, op0=ALU.add, op1=ALU.add))
            for o in range(MORE):
                V.tensor_scalar(is_before[:, o, :], incl[:, :], float(o), None, ALU.is_le)
                ins = V.scalar_tensor_tensor(out=more_before[:, o, :], in0=incl[:, :], scalar=float(o), in1=more_e[:, :],
                                             op0=ALU.is_le, op1=ALU.mult)
            link(ins)
            V.reduce_sum(out=o_tmp[:, 0, :], in_=is_before, axis=AX_X)
            V.reduce_sum(out=o_tmp[:, 1, :], in_=more_before, axis=AX_X)
            link(V.tensor_scalar(o_tmp[:, 2, :], iota_f[:, 0:MORE], incl[:, NE - 1:NE], None, ALU.is_lt))
            link(V.tensor_tensor(v_tab[:, 0, NE:VISITS], o_tmp[:, 0, :], o_tmp[:, 2, :], ALU.mult))
            link(V.tensor_scalar(v_tab[:, 1, NE:VISITS], o_tmp[:, 2, :], float(CLASSES), None, ALU.mult))
            link(V.tensor_tensor(o_tmp[:, 3, :], iota_f[:, 0:MORE], o_tmp[:, 1, :], ALU.subtract))
            link(V.tensor_scalar(o_tmp[:, 3, :], o_tmp[:, 3, :], float(SLOTS), float(SLOTS) - NEVER, ALU.mult, ALU.add))
            link(V.tensor_tensor(o_tmp[:, 3, :], o_tmp[:, 3, :], o_tmp[:, 2, :], ALU.mult))
            link(V.tensor_scalar(v_tab[:, 3, NE:VISITS], o_tmp[:, 3, :], NEVER, None, ALU.add))
            link(V.tensor_copy(v_tab[:, 0, 0:NE], iota_f[:, :]))
            V.memset(v_tab[:, 2, 0:1], 0.0)
            link(V.tensor_copy(v_tab[:, 2, 1:VISITS + 1], v_tab[:, 1, 0:VISITS]))
            link(V.tensor_copy(v_int[:, :, :], v_tab[:, 0:3, :]))
            link(V.tensor_scalar(n_vis[:, :], incl[:, NE - 1:NE], float(NE), None, ALU.add))
            dve.wait_ge(S["blanks_made"], 3)
            V.memset(hit[:, :], 0.0).then_inc(S["tables_ready"], 1)

            def write_list(n):
                e = dve.value_load(v_int[0:1, 0, bass.ds(n, 1)], min_val=0, max_val=NE - 1)
                V.tensor_copy(g_e[:, :, :], g_cols[:, :, bass.ds(e, 1), :].rearrange("p t a n -> p t (a n)"))
                link(V.tensor_scalar(place_e[:, :], place[:, :, bass.ds(e, 1)].rearrange("p t a -> p (t a)"),
                                     v_tab[:, 3, bass.ds(n, 1)], None, ALU.subtract))
                for t in range(TT):
                    ins = V.tensor_scalar(onehot[:, t, :], iota_b[:, :], place_e[:, t:t + 1], None, ALU.is_equal)
                ins.then_inc(S["list_made"], 1)

            def read_list(n):
                dve.wait_ge(S["list_summed"], n + 1)
                link(V.tensor_copy(list_sb[:, :, :], list_ps))
                V.tensor_tensor(look[:, 0, :], list_sb[:, :, 0], list_sb[:, :, 1], ALU.add)
                V.tensor_tensor(list_sb[:, :, 6], slot_id[:, :], list_sb[:, :, 2], ALU.mult)
                link(V.tensor_tensor(look[:, 1, :], list_sb[:, :, 3], list_sb[:, :, 4], ALU.add))
                V.tensor_tensor(list_sb[:, :, 7], slot_id[:, :], list_sb[:, :, 6], ALU.subtract)
                link(V.tensor_tensor(look[:, 1, :], look[:, 1, :], list_sb[:, :, 5], ALU.add))
                link(V.tensor_tensor(look[:, 0, :], look[:, 0, :], list_sb[:, :, 7], ALU.add))
                V.tensor_copy(gather_i[:, :], look[:, 0, :]).then_inc(S["gather_ready"], 1)

            def shift_lists(v):
                dve.wait_ge(S["scattered_a"], v * 16 + 16)
                dve.wait_ge(S["scattered_b"], v * 16 + 16)
                V.tensor_copy(scatter_i[:, :], here[:, 0, :])
                link(V.tensor_copy(gone_g[:, :], here[:, 1, :]))

            def y_out(n, b):
                for h in range(2):
                    i = 2 * b + h
                    dve.wait_ge(S["y_turned"], n * 4 + (i + 1))
                    hs = slice(h * HALF, (h + 1) * HALF)
                    V.scalar_tensor_tensor(out=y_nat[b][:, hs], in0=half(4 + h), scalar=gone_g[:, b:b + 1], in1=gate2_b[:, hs],
                                           op0=ALU.mult, op1=ALU.mult).then_inc(S["y_made"], 1)

            def finish_pair(v, j):
                dve.wait_ge(S["s_made"], v * FT + (j + 1))
                dve.wait_ge(S["t_made"], v * FT + (j + 1))
                V.tensor_tensor(actT[:, j, :], t_buf[:, j % 2, :], s_buf[:, j % 2, :], ALU.mult).then_inc(S["act_made"], 1)

            write_list(0)
            read_list(0)
            for ps in bank:
                V.memset(ps[:, :], 0.0).then_inc(S["pair_read"], 1)
            with dve.Fori(0, VISITS // GROUP) as group:
                at = dve.value_load(v_int[0:1, 1, bass.ds(group * GROUP, 1)], min_val=0, max_val=CLASSES)
                with dve.If(at > 0):
                    with dve.Fori(0, GROUP) as turn:
                        v = group * GROUP + turn
                        cls = dve.value_load(v_int[0:1, 1, bass.ds(v, 1)], min_val=0, max_val=CLASSES)
                        with dve.If(cls > 0):
                            link.loop(v, LINKS_PER_VISIT)
                            e = dve.value_load(v_int[0:1, 0, bass.ds(v, 1)], min_val=0, max_val=NE - 1)
                            shift_lists(v)
                            V.tensor_copy(here[:, :, :], look[:, :, :])
                            link(V.tensor_copy(bias_e[:, :], bgu[:, bass.ds(e, 1), :].rearrange("p a j -> p (a j)")))
                            write_list(v + 1)
                            for j in range(FT):
                                if j in (2, 3):
                                    y_out(v, j - 2)
                                if j == 4:
                                    read_list(v + 1)
                                ps = bank[j % 4]
                                dve.wait_ge(S["pair_summed"], v * FT + (j + 1))
                                V.tensor_scalar(g_buf[:, j % 2, :], ps[:, 0:SLOTS], bias_e[:, j:j + 1], LIMIT, ALU.add,
                                                ALU.min).then_inc(S["g_made"], 1)
                                V.tensor_scalar(u_buf[:, j % 2, :], ps[:, SLOTS:2 * SLOTS], bias_e[:, FT + j:FT + j + 1], LIMIT + 1,
                                                ALU.add, ALU.min).then_inc(S["pair_read"], 1)
                                if j >= 1:
                                    finish_pair(v, j - 1)
                                dve.wait_ge(S["pair_read"], v * FT + (j + 5))
                                V.scalar_tensor_tensor(out=t_buf[:, j % 2, :], in0=u_buf[:, j % 2, :], scalar=1.0 - LIMIT, in1=g_buf[:, j % 2, :],
                                                       op0=ALU.max, op1=ALU.mult).then_inc(S["t_made"], 1)
                            finish_pair(v, FT - 1)
            n = dve.value_load(n_vis[0:1, 0:1], min_val=NE, max_val=VISITS)
            link.end(n)
            shift_lists(n)
            y_out(n, 0)
            y_out(n, 1)
            dve.wait_ge(S["g_final_loaded"], 16)
            for t in range(TT):
                dve.wait_ge(S["fin_rstd"], t + 1)
                V.scalar_tensor_tensor(out=fin[:, t, :], in0=fin[:, t, :], scalar=rstd3[:, t:t + 1], in1=g_fin_b,
                                       op0=ALU.mult, op1=ALU.mult).then_inc(S["fin_made"], 1)

        @block.tensor
        def _(pe):
            M = nc.tensor

            def piece(n):
                pe.wait_ge(dense_loaded[n % RING1], 16 * (n // RING1 + 1))
                return dense_piece(n)

            def product(ps, pairs):
                pairs = list(pairs)
                for i, (w, m) in enumerate(pairs):
                    ins = M.matmul(ps, w, m, start=i == 0, stop=i == len(pairs) - 1)
                return ins

            pe.wait_ge(S["idents_made"], 1)
            pe.wait_ge(S["small_loaded"], 16 * 13)
            M.transpose(bank[0][:, 0:84], row_a[0:84, :], ident[0:84, 0:84])
            M.transpose(bank[0][:, P:P + TAPS * CT], row_c[0:TAPS * CT, :], ident[0:TAPS * CT, 0:TAPS * CT])
            M.transpose(bank[0][:, 2 * P:2 * P + 1], freq_row[0:1, :], ident[0:1, 0:1])
            for q in range(4):
                ins = M.transpose(bank[1][:, q * P:(q + 1) * P], row_g[:, q, :], ident[:, :])
            ins.then_inc(S["rows_turned"], 1)

            def mod_sums(first):
                for i in range(8):
                    w = piece(first + i)
                    product(bank[i // 2][0:1, (i % 2) * PIECE:(i % 2 + 1) * PIECE],
                            ((c_act[:, k:k + 1], w[:, k, :]) for k in range(KD))).then_inc(S["mod_summed"], 1)

            def turn_mod(copied):
                pe.wait_ge(S["mod_copied"], copied)
                for col in range(2 * KD):
                    ins = M.transpose(bank[2][:, col:col + 1], mod_row[:, col * P:(col + 1) * P], ident[0:1, 0:1])
                ins.then_inc(S["mod_turned"], 1)

            def mod_rows(first):
                for i in range(4):
                    w = piece(first + i)
                    product(wide[0][:, i * PIECE:(i + 1) * PIECE], ((c_bc[:, k, :], w[:, k, :]) for k in range(KD))).then_inc(S["gates_summed"], 1)

            pe.wait_ge(S["c_ready"], 1)
            mod_sums(0)
            turn_mod(4)
            for n in range(2 * KD):
                g, k = n // KD, n % KD
                pe.wait_ge(S["x_scaled"], 4 * (g + 1))
                if n < 4:
                    pe.wait_ge(S["scale1_made"], 1)
                else:
                    pe.wait_ge(S["h_even" if n % 2 == 0 else "h_odd"], n // 2 - 1)
                for j in range(4):
                    ins = M.transpose(half(n % 4)[:, j * P:(j + 1) * P], x_in[:, 4 * g + j, k * P:(k + 1) * P], ident[:, :])
                ins.then_inc(S["x_turned"], 1)
            pe.wait_ge(S["h_even"], KD)
            pe.wait_ge(S["h_odd"], KD)
            for i in range(2 * CT):
                ct, h = i // 2, i % 2
                for j in range(2):
                    w = piece(AG + 2 * (ct // 2) + j)
                    if i >= 2:
                        pe.wait_ge(S["sig_made" if j else "a_copied"], i - 1)
                    if i == 0:
                        pe.wait_ge(S["zeros_made"], 1)
                    product(half(4 + (2 * i + j) % 4), ((w[:, k, (ct % 2) * P:(ct % 2 + 1) * P], hT[:, k, h * HALF:(h + 1) * HALF])
                                                        for k in range(KD))).then_inc(S["ag_summed"], 1)
            for i in range(4 * QT):
                f, h = i // 2, i % 2
                w = piece(QK + f // 2)
                if i >= 2:
                    pe.wait_ge(S["qkv_copied"], i - 1)
                product(half(i % 2), ((w[:, k, (f % 2) * P:(f % 2 + 1) * P], hT[:, k, h * HALF:(h + 1) * HALF])
                                      for k in range(KD))).then_inc(S["qkv_summed"], 1)
            for t in range(TT):
                pe.wait_ge(S["qkv_copied"], 4 * QT + t - 1)
                for j in range(2):
                    w = piece(QK + 4 + j)
                    ins = product(half(t % 2)[:, j * PIECE:(j + 1) * PIECE], ((hT[:, k, t * P:(t + 1) * P], w[:, k, :]) for k in range(KD)))
                ins.then_inc(S["qkv_summed"], 1)
                for i in (2 * t, 2 * t + 1):
                    src, f = (qT, i // 2) if i < 2 * QT else (kT, i // 2 - QT)
                    pe.wait_ge(S["qkv_copied"], i + 1)
                    if i >= 2:
                        pe.wait_ge(S["rot_read"], i - 1)
                    M.matmul(half(2 + i % 2), rot_m[:, :], src[:, f, (i % 2) * HALF:(i % 2 + 1) * HALF], start=True,
                             stop=True).then_inc(S["rot_summed"], 1)
                if t == 4:
                    pe.wait_ge(S["conv_made"], CT)
                    pe.wait_ge(S["sig_made"], 2 * CT)
                    for h in range(2):
                        product(half(4 + h), ((ones[:, :], conv[:, ct, h * HALF:(h + 1) * HALF]) for ct in range(CT))).then_inc(S["mean_summed"], 1)
                for i in variances_after.get(t, ()):
                    h, ct = i // CT, i % CT
                    pe.wait_ge(S["squared"], i + 1)
                    M.matmul(half(6 + h), ones[:, :], norm_tmp[2 + i % 2][:, 0:HALF], start=ct == 0, stop=ct == CT - 1).then_inc(S["var_summed"], 1)
            pe.wait_ge(S["c_spread"], 1)
            pe.wait_ge(S["centred"], 2 * CT)
            mod_rows(ADA2)
            pe.wait_ge(S["q_rotated"], 4 * QT)
            pe.wait_ge(S["qkv_copied"], 4 * QT + TT)
            mod_sums(ADA2 + 4)
            pe.wait_ge(S["gate_made"], 1)
            mod_rows(ADA2 + 12)
            turn_mod(8)

            ITEMS = TT * HEADS

            def score(i):
                qt, h = i // HEADS, i % HEADS
                n, rows_h = (qt + 1) * P, slice((h % 2) * HD, (h % 2 + 1) * HD)
                if i >= 2:
                    pe.wait_ge(S["score_masked"], i - 1)
                for at in range(0, n, HALF):
                    m = min(HALF, n - at)
                    ins = M.matmul(wide[i % 2][:, at:at + m], qT[rows_h, h // 2, qt * P:(qt + 1) * P], kT[rows_h, h // 2, at:at + m],
                                   start=True, stop=True)
                ins.then_inc(S["scored"], 1)

            def turn(i):
                pe.wait_ge(S["exped"], i + 1)
                if i >= 1:
                    pe.wait_ge(S["probT_act"], i)
                    if i - 1 >= 4 * HEADS:
                        pe.wait_ge(S["probT_dve"], i - 4 * HEADS)
                for kt in range(i // HEADS + 1):
                    ins = M.transpose(half(kt // 4)[:, (kt % 4) * P:(kt % 4 + 1) * P], prob[i % 2][:, kt * P:(kt + 1) * P], ident[:, :])
                ins.then_inc(S["prob_turned"], 1)

            def weigh(i):
                qt, h = i // HEADS, i % HEADS
                pe.wait_ge(S["probT_act"], i + 1)
                if qt >= 4:
                    pe.wait_ge(S["probT_dve"], i - 4 * HEADS + 1)
                if i >= 2:
                    pe.wait_ge(S["o_made"], i - 1)
                if h == 3 and qt >= 1:
                    turn_attn(qt - 1, i - 1)
                    pe.wait_ge(S["attn_made"], qt)
                product(half(2 + i % 2)[:, h * HD:(h + 1) * HD], ((probT[i % 2][:, kt * P:(kt + 1) * P], v_nat[:, kt, h * HD:(h + 1) * HD])
                                                          for kt in range(qt + 1))).then_inc(S["weighed"], 1)

            def turn_attn(qt, made):
                pe.wait_ge(S["o_made"], made)
                for f in range(QT):
                    ins = M.transpose(half(3)[:, f * P:(f + 1) * P], o_nat[qt % 2][:, f * P:(f + 1) * P], ident[:, :])
                ins.then_inc(S["attn_turned"], 1)

            pe.wait_ge(S["scale2_made"], 1)
            pe.wait_ge(S["gate_made"], 2)
            pe.wait_ge(S["qkv_copied"], 4 * QT + TT)
            score(0)
            score(1)
            for i in range(ITEMS):
                turn(i)
                if i + 2 < ITEMS:
                    score(i + 2)
                weigh(i)
            turn_attn(TT - 1, ITEMS)

            mixT = [conv[:, ct, :] for ct in range(CT)] + [attnT[:, f, :] for f in range(QT)]
            pe.wait_ge(S["conv_out"], CT)
            pe.wait_ge(S["attn_made"], TT)
            pe.wait_ge(S["b_down_loaded"], 16)
            pe.wait_ge(S["consts_made"], 1)
            for t in range(TT + 2):
                if t < TT:
                    if t >= 1:
                        pe.wait_ge(S["mix_read"], t)
                    for i in range(4):
                        w = piece(OUT + i)
                        ins = product(wide[0][:, i * PIECE:(i + 1) * PIECE], ((mixT[k][:, t * P:(t + 1) * P], w[:, k, :]) for k in range(KD)))
                    ins.then_inc(S["mixed"], 1)
                if t >= 2:
                    s = t - 2
                    pe.wait_ge(S["picked_made"], s + 1)
                    M.transpose(bank[3][0:NE, P:2 * P], gates[:, s, :], ident[:, :])
                    product(bank[3][:, 2 * P:2 * P + NE], ((before_m[:, :], picked_b[:, s % 2, :]),
                                                           (ones_b[:, :], so_far_b[:, s % 2, :]))).then_inc(S["placed"], 1)
                if 1 <= t <= TT:
                    s = t - 1
                    pe.wait_ge(S["xn_made"], s + 1)
                    if s >= 1:
                        pe.wait_ge(S["h2_low"], s)
                        pe.wait_ge(S["h2_high"], s)
                    for k in range(KD):
                        ins = M.transpose(wide[1][:, k * P:(k + 1) * P], xn1[:, k * P:(k + 1) * P], ident[:, :])
                    ins.then_inc(S["xn_turned"], 1)
                if t >= 2:
                    s = t - 2
                    pe.wait_ge(S["gatesT_made"], s + 1)
                    if s >= 1:
                        pe.wait_ge(S["bd_read"], 2 * s)
                    for h in range(2):
                        M.matmul(half(1 + h), gatesT[:, :], b_down_sb[:, h * HALF:(h + 1) * HALF], start=True, stop=True).then_inc(S["bd_summed"], 1)
                if 1 <= t <= TT:
                    s = t - 1
                    pe.wait_ge(S["h2_low"], s + 1)
                    pe.wait_ge(S["h2_high"], s + 1)
                    product(bank[0][:, 0:NE], ((h2T[s % 2][:, k, :], wr[:, k, :]) for k in range(KD))).then_inc(S["logits_summed"], 1)
            pe.wait_ge(S["picked_made"], TT + 1)
            M.matmul(bank[3][:, 3 * P:3 * P + NE], ones_b[:, :], so_far_b[:, 0, :], start=True, stop=True).then_inc(S["counted"], 1)

            def make_list(n):
                pe.wait_ge(S["list_made"], n + 1)
                for b in range(2):
                    ins = product(list_ps[:, b, :], ((onehot[:, t, b * P:(b + 1) * P], g_e[:, t, :]) for t in range(TT)))
                ins.then_inc(S["list_summed"], 1)

            def turn_x(n, parts, tiles, first=False):
                for q in parts:
                    if q >= 2:
                        pe.wait_ge(S["x2_made"], n * 4 + (q - 1))
                    elif not first:
                        pe.wait_ge(S["y_made"], n * 4 + (q - 1))
                    for k in (2 * q, 2 * q + 1):
                        for b in range(tiles):
                            at = (k % 4) * SLOTS + b * P
                            ins = M.transpose(wide[0][:, at:at + P], got[b][:, k * P:(k + 1) * P], ident[:, :])
                    ins.then_inc(S["x2_turned"], 1)

            def gathered(n):
                pe.wait_ge(S["gathered_a"], n * 16 + 16)
                pe.wait_ge(S["gathered_b"], n * 16 + 16)

            def turn_next(v, following, parts):
                with pe.If(following <= FEW_CLASSES):
                    turn_x(v + 1, parts, 1)
                with pe.Else():
                    turn_x(v + 1, parts, 2)

            def outputs_copied(n):
                pe.wait_ge(S["y_copied"], n * KD + 2)
                pe.wait_ge(S["x2_made"], n * 4 + 4)

            def turn_y(n, b):
                for h in range(2):
                    i = 2 * b + h
                    if i >= 2:
                        pe.wait_ge(S["y_made"], n * 4 + (i - 1))
                    for m in range(4):
                        ins = M.transpose(half(4 + h)[:, m * P:(m + 1) * P], yT[:, 4 * h + m, b * P:(b + 1) * P], ident[:, :])
                    ins.then_inc(S["y_turned"], 1)

            def visit(v, n):
                for j in range(FT):
                    if j == 0:
                        pe.wait_ge(S["x2_made"], v * 4 + 4)
                    if j == 2:
                        outputs_copied(v)
                        turn_y(v, 0)
                    if j == 3:
                        before = pe.value_load(v_int[0:1, 2, bass.ds(v, 1)], min_val=0, max_val=CLASSES)
                        with pe.If(before <= FEW_CLASSES):
                            pe.wait_ge(S["y_made"], v * 4 + 2)
                            M.transpose(half(5)[:, 0:P], yT[:, 4, P:2 * P], ident[:, :]).then_inc(S["y_turned"], 2)
                        with pe.Else():
                            turn_y(v, 1)
                    if j == 4:
                        make_list(v + 1)
                    if j % 2 == 0:
                        pe.wait_ge(piece_loaded[j], v * 16 + 16)
                        pe.wait_ge(piece_loaded[j + 1], v * 16 + 16)
                    pe.wait_ge(S["pair_read"], v * FT + (j + 1))
                    for half_p in range(2):
                        w = ring[:, ring_slot(2 * (j // 2) + half_p)]
                        ins = product(bank[j % 4][:, half_p * SLOTS:half_p * SLOTS + n],
                                      ((w[:, k, (j % 2) * P:(j % 2 + 1) * P], xT[:, k, 0:n]) for k in range(KD)))
                    ins.then_inc(S["pair_summed"], 1)
                gathered(v + 1)
                following = pe.value_load(v_int[0:1, 1, bass.ds(v + 1, 1)], min_val=0, max_val=CLASSES)
                turn_next(v, following, (0, 1))
                for m in range(KD):
                    if m % 2 == 0:
                        pe.wait_ge(piece_loaded[8 + m // 2], v * 16 + 16)
                    pe.wait_ge(S["y_copied"], v * KD + (m + 1))
                    if m == 1:
                        pe.wait_ge(S["gather_ready"], v + 2)
                    w = ring[:, ring_slot(8 + m // 2)]
                    for k in range(FT):
                        if m == 0 and k in (0, FT - 2, FT - 1):
                            pe.wait_ge(S["act_made"], v * FT + max(k + 1, FT - 2))
                        ins = M.matmul(half(6 + m % 2)[:, 0:n], w[:, k, (m % 2) * P:(m % 2 + 1) * P], actT[:, k, 0:n],
                                       start=k == 0, stop=k == FT - 1)
                    ins.then_inc(S["y_summed"], 1)
                    if m == 0:
                        turn_next(v, following, (2, 3))

            def choose(v, cls, low, high):
                if low == high:
                    visit(v, WIDTHS[low - 1])
                    return
                middle = (low + high) // 2
                with pe.If(cls <= middle):
                    choose(v, cls, low, middle)
                with pe.Else():
                    choose(v, cls, middle + 1, high)

            pe.wait_ge(S["tables_ready"], 1)
            pe.wait_ge(S["consts_made"], 2)
            make_list(0)
            gathered(0)
            turn_x(0, range(4), 2, first=True)
            with pe.Fori(0, VISITS // GROUP) as group:
                at = pe.value_load(v_int[0:1, 1, bass.ds(group * GROUP, 1)], min_val=0, max_val=CLASSES)
                with pe.If(at > 0):
                    with pe.Fori(0, GROUP) as turn:
                        v = group * GROUP + turn
                        cls = pe.value_load(v_int[0:1, 1, bass.ds(v, 1)], min_val=0, max_val=CLASSES)
                        with pe.If(cls > 0):
                            choose(v, cls, 1, CLASSES)
            n = pe.value_load(n_vis[0:1, 0:1], min_val=NE, max_val=VISITS)
            outputs_copied(n)
            turn_y(n, 0)
            turn_y(n, 1)


_IN = ("x", "c", "positions", "w_ada", "b_ada", "g_mix", "w_in", "conv_w", "conv_b", "conv_ln_g", "conv_ln_b", "w_out", "g_ffn",
       "w_router", "b_router", "w_gu", "b_gu", "w_down", "b_down", "g_final")
_SHAPES = {"x": (T, D), "w_ada": (D, 6 * D), "w_in": (D, 2 * CH + 3 * HEADS * HD), "w_out": (D, D), "w_router": (D, NE),
           "w_gu": (NE, D, 2 * D), "w_down": (NE, D, D), "b_down": (NE, D)}


def kernel(**inputs):
    import concourse.bacc as bacc
    from concourse.bass_utils import run_bass_kernel_spmd

    nc = bacc.Bacc("TRN2", target_bir_lowering=False, num_devices=1)
    arrays, views = {}, []
    for name in _IN:
        a = np.asarray(inputs[name])
        a = np.ascontiguousarray(a.reshape(_SHAPES.get(name, (-1,))))
        arrays[f"in_{name}"] = a
        views.append(nc.dram_tensor(f"in_{name}", a.shape, mybir.dt.from_np(a.dtype), kind="ExternalInput").ap())
    out = nc.dram_tensor("out", (T, D), F32, kind="ExternalOutput").ap()
    decoder_layer(nc, *views, out)
    result = run_bass_kernel_spmd(nc, [arrays], core_ids=[0])
    return result.results[0]["out"].reshape(1, T, D)
```
